# Optimizing a Trainium2 kernel written in Bass

```python
import jax, jax.numpy as jnp
from jax import lax
import numpy as np

D_MODEL = 1024
BATCH = 1
SEQ = 1024
DEPTH = 2
DEC_BATCH = 8
DEC_SEQ = 16
PAST_LEN = 512

CHUNK = 64
N_LEFT_CHUNKS = 8
BAND_PAST = N_LEFT_CHUNKS * CHUNK
A_HEADS = 8
A_HEAD_DIM = 64
A_WIDTH = A_HEADS * A_HEAD_DIM
MAX_REL = 128
B_WIDTH = D_MODEL - A_WIDTH
CONV_WIDTH = 31
C_HEADS = 8
C_KEY_DIM = 128
C_VAL_DIM = D_MODEL // C_HEADS
C_WIDTH = C_HEADS * C_VAL_DIM
D_FF = ((8 * D_MODEL // 3 + 255) // 256) * 256
N_EVEN = (DEPTH + 1) // 2
N_ODD = DEPTH // 2
EPS = 1e-6
NEG = -1e30

kernel_name = "hybrid_chunk_stream_encoder_step"

def rmsnorm(x, g):
    xf = x.astype(jnp.float32)
    y = xf * lax.rsqrt(jnp.mean(xf * xf, axis=-1, keepdims=True) + EPS)
    return (y * g.astype(jnp.float32)).astype(x.dtype)

def layernorm(x, g, b):
    xf = x.astype(jnp.float32)
    mu = jnp.mean(xf, axis=-1, keepdims=True)
    var = jnp.mean(jnp.square(xf - mu), axis=-1, keepdims=True)
    y = (xf - mu) * lax.rsqrt(var + EPS)
    return (y * g.astype(jnp.float32) + b.astype(jnp.float32)).astype(x.dtype)

def rel_bias_lookup(rel_bias, rel):
    return rel_bias[:, jnp.clip(rel, -MAX_REL, MAX_REL) + MAX_REL].astype(jnp.float32)

def band_attention_prompt(q, k, v, rel_bias):
    Bsz, T, H, Dh = q.shape
    nc = T // CHUNK
    band = BAND_PAST + CHUNK
    kp = jnp.pad(k, ((0, 0), (BAND_PAST, 0), (0, 0), (0, 0)))
    vp = jnp.pad(v, ((0, 0), (BAND_PAST, 0), (0, 0), (0, 0)))
    qc = q.reshape(Bsz, nc, CHUNK, H, Dh).swapaxes(0, 1)
    offs_q = jnp.arange(CHUNK)
    offs_k = jnp.arange(band)
    bias = rel_bias_lookup(rel_bias, offs_q[:, None] + BAND_PAST - offs_k[None, :])
    scale = A_HEAD_DIM ** -0.5

    def one_chunk(args):
        c, qb = args
        start = c * CHUNK
        kb = lax.dynamic_slice_in_dim(kp, start, band, axis=1)
        vb = lax.dynamic_slice_in_dim(vp, start, band, axis=1)
        valid = (start - BAND_PAST + offs_k) >= 0
        s = jnp.einsum('bqhd,bkhd->bhqk', qb, kb).astype(jnp.float32) * scale + bias[None]
        s = jnp.where(valid[None, None, None, :], s, NEG)
        p = jax.nn.softmax(s, axis=-1).astype(vb.dtype)
        return jnp.einsum('bhqk,bkhd->bqhd', p, vb)

    out = lax.map(one_chunk, (jnp.arange(nc), qc))
    return out.swapaxes(0, 1).reshape(Bsz, T, H, Dh)

def band_attention_sample(q, k_new, v_new, k_cache, v_cache, rel_bias):
    W = k_cache.shape[1]
    L = q.shape[1]
    k = jnp.concatenate([k_cache.astype(k_new.dtype), k_new], axis=1)
    v = jnp.concatenate([v_cache.astype(v_new.dtype), v_new], axis=1)
    rel = (W + jnp.arange(L))[:, None] - jnp.arange(W + L)[None, :]
    bias = rel_bias_lookup(rel_bias, rel)
    s = jnp.einsum('bqhd,bkhd->bhqk', q, k).astype(jnp.float32) * (A_HEAD_DIM ** -0.5) + bias[None]
    p = jax.nn.softmax(s, axis=-1).astype(v.dtype)
    return jnp.einsum('bhqk,bkhd->bqhd', p, v)

def conv_module(pre_glu, conv_hist, conv_w, conv_b, ln_g, ln_b):
    a, g = jnp.split(pre_glu, 2, axis=-1)
    u = a * jax.nn.sigmoid(g)
    u_ext = jnp.concatenate([conv_hist.astype(u.dtype), u], axis=1)
    y = lax.conv_general_dilated(u_ext, conv_w[:, None, :].astype(u.dtype), window_strides=(1,),
                                 padding='VALID', dimension_numbers=('NWC', 'WIO', 'NWC'),
                                 feature_group_count=B_WIDTH) + conv_b
    y = jax.nn.silu(layernorm(y, ln_g, ln_b))
    return y, u_ext[:, -(CONV_WIDTH - 1):]

def mixer_ab(h, k_cache, v_cache, conv_hist, w_in, rel_bias, conv_w, conv_b, ln_g, ln_b, w_out):
    Bsz, T, _ = h.shape
    z = h @ w_in
    q = z[..., :A_WIDTH].reshape(Bsz, T, A_HEADS, A_HEAD_DIM)
    k = z[..., A_WIDTH:2 * A_WIDTH].reshape(Bsz, T, A_HEADS, A_HEAD_DIM)
    v = z[..., 2 * A_WIDTH:3 * A_WIDTH].reshape(Bsz, T, A_HEADS, A_HEAD_DIM)
    pre_glu = z[..., 3 * A_WIDTH:]
    if k_cache is None:
        att = band_attention_prompt(q, k, v, rel_bias)
        keep = min(BAND_PAST, T)
        new_k, new_v = k[:, T - keep:], v[:, T - keep:]
        conv_hist = jnp.zeros((Bsz, CONV_WIDTH - 1, B_WIDTH), h.dtype)
    else:
        att = band_attention_sample(q, k, v, k_cache, v_cache, rel_bias)
        new_k, new_v = k, v
    conv_out, new_hist = conv_module(pre_glu, conv_hist, conv_w, conv_b, ln_g, ln_b)
    out = jnp.concatenate([att.reshape(Bsz, T, A_WIDTH), conv_out], axis=-1) @ w_out
    return out, new_k, new_v, new_hist

def hgrn2_chunk(S, q, k, v, logf):
    L = q.shape[1]
    G = jnp.cumsum(logf, axis=1)
    causal = jnp.tril(jnp.ones((L, L), dtype=bool))
    diff = G[:, :, None] - G[:, None, :]
    decay = jnp.exp(jnp.where(causal[None, :, :, None, None], diff, -jnp.inf))
    A = jnp.einsum('bthk,bshk,btshk->bhts', q, k, decay)
    o = jnp.einsum('bhts,bshv->bthv', A, v) + jnp.einsum('bthk,bhkv->bthv', q * jnp.exp(G), S)
    GL = G[:, -1]
    kd = k * jnp.exp(GL[:, None] - G)
    S_new = jnp.exp(GL)[..., None] * S + jnp.einsum('bshk,bshv->bhkv', kd, v)
    return S_new, o

def mixer_c(h, S0, w_in, lb, gn_g, w_out):
    Bsz, T, _ = h.shape
    z = h @ w_in
    qx, fx, ix, gx = jnp.split(z, 4, axis=-1)
    hk = (Bsz, T, C_HEADS, C_KEY_DIM)
    q = qx.reshape(hk).astype(jnp.float32)
    f = lb + (1.0 - lb) * jax.nn.sigmoid(fx.reshape(hk).astype(jnp.float32))
    logf = jnp.log(f)
    k = 1.0 - f
    v = ix.reshape(Bsz, T, C_HEADS, C_VAL_DIM).astype(jnp.float32)
    if S0 is None:
        nc = T // CHUNK

        def to_chunks(a):
            return a.reshape(Bsz, nc, CHUNK, *a.shape[2:]).swapaxes(0, 1)

        def step(S, xs):
            qc, kc, vc, lc = xs
            return hgrn2_chunk(S, qc, kc, vc, lc)

        S_init = jnp.zeros((Bsz, C_HEADS, C_KEY_DIM, C_VAL_DIM), jnp.float32)
        S, o = lax.scan(step, S_init, (to_chunks(q), to_chunks(k), to_chunks(v), to_chunks(logf)))
        o = o.swapaxes(0, 1).reshape(Bsz, T, C_HEADS, C_VAL_DIM)
    else:
        S, o = hgrn2_chunk(S0.astype(jnp.float32), q, k, v, logf)
    o = rmsnorm(o, gn_g).reshape(Bsz, T, C_WIDTH).astype(h.dtype) * jax.nn.silu(gx)
    return o @ w_out, S.astype(h.dtype)

def swiglu(h, w_in, w_out):
    a, b = jnp.split(h @ w_in, 2, axis=-1)
    return (jax.nn.silu(a) * b) @ w_out

def setup_inputs(seed: int = 0) -> dict:
    key = jax.random.key(seed)
    ks = jax.random.split(key, 24)
    f32 = jnp.float32
    nrm = lambda k, shp, s: jax.random.normal(k, shp, f32) * s
    wa = min(BAND_PAST, PAST_LEN)
    return {
        "x_prompt": nrm(ks[0], (BATCH, SEQ, D_MODEL), 1.0),
        "x_sample": nrm(ks[1], (DEC_BATCH, DEC_SEQ, D_MODEL), 1.0),
        "cache_a_k": nrm(ks[2], (N_EVEN, DEC_BATCH, wa, A_HEADS, A_HEAD_DIM), 1.0),
        "cache_a_v": nrm(ks[3], (N_EVEN, DEC_BATCH, wa, A_HEADS, A_HEAD_DIM), 1.0),
        "state_conv": nrm(ks[4], (N_EVEN, DEC_BATCH, CONV_WIDTH - 1, B_WIDTH), 0.5),
        "state_hgrn": nrm(ks[5], (N_ODD, DEC_BATCH, C_HEADS, C_KEY_DIM, C_VAL_DIM), 0.5),
        "attn_norm": 1.0 + nrm(ks[6], (DEPTH, D_MODEL), 0.02),
        "ffn_norm": 1.0 + nrm(ks[7], (DEPTH, D_MODEL), 0.02),
        "final_norm": 1.0 + nrm(ks[8], (D_MODEL,), 0.02),
        "w_in_ab": nrm(ks[9], (N_EVEN, D_MODEL, 3 * A_WIDTH + 2 * B_WIDTH), D_MODEL ** -0.5),
        "rel_bias": nrm(ks[10], (N_EVEN, A_HEADS, 2 * MAX_REL + 1), 0.1),
        "conv_w": nrm(ks[11], (N_EVEN, CONV_WIDTH, B_WIDTH), CONV_WIDTH ** -0.5),
        "conv_b": nrm(ks[12], (N_EVEN, B_WIDTH), 0.02),
        "conv_ln_g": 1.0 + nrm(ks[13], (N_EVEN, B_WIDTH), 0.02),
        "conv_ln_b": nrm(ks[14], (N_EVEN, B_WIDTH), 0.02),
        "w_out_ab": nrm(ks[15], (N_EVEN, D_MODEL, D_MODEL), D_MODEL ** -0.5),
        "w_in_c": nrm(ks[16], (N_ODD, D_MODEL, 4 * C_WIDTH), D_MODEL ** -0.5),
        "lower_bounds": nrm(ks[17], (DEPTH, C_HEADS * C_KEY_DIM), 1.0),
        "c_norm_g": 1.0 + nrm(ks[18], (N_ODD, C_VAL_DIM), 0.02),
        "w_out_c": nrm(ks[19], (N_ODD, C_WIDTH, D_MODEL), C_WIDTH ** -0.5),
        "ffn_w_in": nrm(ks[20], (DEPTH, D_MODEL, 2 * D_FF), D_MODEL ** -0.5),
        "ffn_w_out": nrm(ks[21], (DEPTH, D_FF, D_MODEL), D_FF ** -0.5),
    }

def reference(x_prompt, x_sample, cache_a_k, cache_a_v, state_conv, state_hgrn,
              attn_norm, ffn_norm, final_norm, w_in_ab, rel_bias, conv_w, conv_b,
              conv_ln_g, conv_ln_b, w_out_ab, w_in_c, lower_bounds, c_norm_g, w_out_c,
              ffn_w_in, ffn_w_out):
    lb_all = jnp.cumsum(jax.nn.softmax(lower_bounds.astype(jnp.float32), axis=0), axis=0)
    lb_all = lb_all - lb_all[0]
    yp, ys = x_prompt, x_sample
    akp, avp, cvp, hgp = [], [], [], []
    aks, avs, cvs, hgs = [], [], [], []
    for li in range(DEPTH):
        hp = rmsnorm(yp, attn_norm[li])
        hs = rmsnorm(ys, attn_norm[li])
        if li % 2 == 0:
            e = li // 2
            wts = (w_in_ab[e], rel_bias[e], conv_w[e], conv_b[e], conv_ln_g[e], conv_ln_b[e], w_out_ab[e])
            mp, kp_, vp_, cp_ = mixer_ab(hp, None, None, None, *wts)
            ms, ks_, vs_, cs_ = mixer_ab(hs, cache_a_k[e], cache_a_v[e], state_conv[e], *wts)
            akp.append(kp_); avp.append(vp_); cvp.append(cp_)
            aks.append(ks_); avs.append(vs_); cvs.append(cs_)
        else:
            o = li // 2
            lb = lb_all[li].reshape(C_HEADS, C_KEY_DIM)
            mp, sp_ = mixer_c(hp, None, w_in_c[o], lb, c_norm_g[o], w_out_c[o])
            ms, ss_ = mixer_c(hs, state_hgrn[o], w_in_c[o], lb, c_norm_g[o], w_out_c[o])
            hgp.append(sp_); hgs.append(ss_)
        yp = yp + mp
        ys = ys + ms
        yp = yp + swiglu(rmsnorm(yp, ffn_norm[li]), ffn_w_in[li], ffn_w_out[li])
        ys = ys + swiglu(rmsnorm(ys, ffn_norm[li]), ffn_w_in[li], ffn_w_out[li])
    y_prompt = rmsnorm(yp, final_norm)
    y_sample = rmsnorm(ys, final_norm)
    return (y_prompt, y_sample,
            jnp.stack(akp), jnp.stack(avp), jnp.stack(cvp), jnp.stack(hgp),
            jnp.stack(aks), jnp.stack(avs), jnp.stack(cvs), jnp.stack(hgs))


_drawn_inputs = setup_inputs


def setup_inputs(seed=0):
    import zlib

    import numpy as np

    out = dict(_drawn_inputs(seed))
    spreads = {}
    factors = {'final_norm': 8.944,
     'rel_bias': 6.801,
     'conv_ln_g': 3.891,
     'conv_ln_b': 3.675,
     'c_norm_g': 21.923,
     'ffn_norm': 3.581}
    for name, (base, spread) in spreads.items():
        noise = np.random.default_rng([zlib.crc32(name.encode()), seed]).standard_normal(out[name].shape)
        drawn = base * np.exp(spread * noise) if base else spread * noise
        out[name] = __import__('jax').numpy.asarray(drawn.astype(out[name].dtype))
    for name, factor in factors.items():
        out[name] = (out[name] * factor).astype(out[name].dtype)
    return out
```

```python
import numpy as np
from contextlib import ExitStack

import concourse.bass as bass
from concourse import mybir

F32 = mybir.dt.float32
F32R = mybir.dt.float32r
I32 = mybir.dt.int32
U8 = mybir.dt.uint8
ALU = mybir.AluOpType
ACT = mybir.ActivationFunctionType
AX = mybir.AxisListType

P = 128
D = 1024
KT = D // P
SEQ = 1024
NB = 8
NS = 16
TOK = SEQ + NB * NS
NT = TOK // P
PT_TILES = SEQ // P
TH = 384
N3 = TOK // TH
TPT = TH // P
AH, AD = 8, 64
AW = AH * AD
AB = AW // P
CACHE = 512
CW = 31
HIST = CW - 1
CH = 8
FF = 2816
FJ = FF // P
NCH = FJ // 2
EPS = 1e-6
NEG = -1e30
LEVELS = 7
SLEVELS = 4
SMALL = dict(cw=(0, AB * CW), cb=(124, AB), lg=(128, AB), lb=(132, AB), gain=(136, 5 * KT),
             low=(176, 2 * CH), gn=(192, 1))
NSMALL = 193


class Tally:

    def __init__(self):
        self.base, self.now, self.step, self.i = {}, {}, {}, None

    def __call__(self, name):
        n = self.base.get(name, 0) + self.now.get(name, 0)
        if self.i is not None and self.step.get(name, 0):
            return self.i * self.step[name] + n
        return n

    def add(self, name, k=1):
        self.now[name] = self.now.get(name, 0) + k

    def enter(self, i, **step):
        for k, v in self.now.items():
            self.base[k] = self.base.get(k, 0) + v
        self.now, self.step, self.i = {}, step, i

    def leave(self, times):
        assert {k: v for k, v in self.now.items() if v} == {k: v for k, v in self.step.items() if v}, (self.now, self.step)
        for k, v in self.step.items():
            self.base[k] = self.base.get(k, 0) + v * times
        self.now, self.step, self.i = {}, {}, None


def need(eng, sem, value):
    if isinstance(value, int) and value <= 0:
        return
    eng.wait_ge(sem, value)


def encoder(nc, x_t, w_ab, w_oab, w_c, w_oc, w_fi, w_fo, small_d, rel_d, kc_d, vc_d, hist_d, state_d,
            y_o, k_o, v_o, cvp_o, cvs_o, hgp_o, hgs_o):
    with ExitStack() as ctx:
        sb = lambda name, shape, dt=F32: ctx.enter_context(nc.sbuf_tensor(name, shape, dt))
        sem = lambda name: ctx.enter_context(nc.semaphore(name))

        X = sb("X", [P, KT, TOK])
        HAH = sb("HAH", [P, AB, TOK], F32R)
        HAL = sb("HAL", [P, AB, TOK], F32R)
        with nc.sbuf_tensor("CACHES", [P, KT * TOK], F32) as CACHES:
            pass
        HBH = sb("HBH", [P, AB, TOK], F32R)
        HBL = sb("HBL", [P, AB, TOK], F32R)
        WR = sb("WR", [P, 3, D])
        WH = sb("WH", [P, 3, D], F32R)
        WL = sb("WL", [P, 3, D], F32R)
        small = sb("small", [P, NSMALL])
        ident = sb("ident", [P, P])
        ones = sb("ones", [P, P])
        lvl_mask = sb("lvl_mask", [P, LEVELS, P], U8)
        low = sb("low", [P, 6, CH])
        parity_i = sb("parity_i", [P, 3], I32)
        parity = sb("parity", [P, 2])
        rt = sb("rt", [P, 16])
        ri = sb("ri", [P, 16])
        nmax = sb("nmax", [P, 2])
        rmax = sb("rmax", [P, 2])
        psum_ = sb("psum_", [P, 4])
        rsum = sb("rsum", [P, 2])
        sums = sb("sums", [P, 2, AH])
        rsums = sb("rsums", [P, AH])
        late = sb("late", [1, P])
        minus = sb("minus", [1, 64])
        eps = sb("eps", [P, 1])
        with ExitStack() as c2:
            s2 = lambda name, shape, dt=F32: c2.enter_context(nc.sbuf_tensor(name, shape, dt))
            SQ = s2("SQ", [P, KT, TH])
            HF = s2("HF", [P, KT, TH])
            DG = s2("DG", [P, TPT, P])
        with ExitStack() as c2:
            s2 = lambda name, shape, dt=F32: c2.enter_context(nc.sbuf_tensor(name, shape, dt))
            VTOK = s2("VTOK", [P, NT, AW])
            Y = s2("Y", [P, AB, TOK])
            with ExitStack() as c3:
                s3 = lambda name, shape, dt=F32: c3.enter_context(nc.sbuf_tensor(name, shape, dt))
                EV = s3("EV", [P, N3, TH])
                UP = s3("UP", [P, HIST + SEQ])
                US = s3("US", [P, AB, NB, HIST + NS])
                CO = s3("CO", [P, AB, HIST])
            BT = s2("BT", [P, AH, 2 * P])
            PR = s2("PR", [P, 2, 5 * P])
            PRT = s2("PRT", [P, 2, 5 * P])
            BS = s2("BS", [P, P + NS])
        with ExitStack() as c2:
            s2 = lambda name, shape, dt=F32: c2.enter_context(nc.sbuf_tensor(name, shape, dt))
            UH = s2("UH", [P, 2, 2, TOK], F32R)
            UL = s2("UL", [P, 2, 2, TOK], F32R)
            SG = s2("SG", [P, N3, TH])
            UF = s2("UF", [P, N3, TH])
        with ExitStack() as c2:
            s2 = lambda name, shape, dt=F32: c2.enter_context(nc.sbuf_tensor(name, shape, dt))
            FG = s2("FG", [P, 2, TOK])
            QC = s2("QC", [P, 2, TOK])
            VC = s2("VC", [P, 2, NT, P])
            KC = s2("KC", [P, TOK])
            AM = s2("AM", [P, NT, P])
            TA = s2("TA", [P, TOK // 2])
            TB = s2("TB", [P, TOK // 4])
            TS = s2("TS", [P, 2 * NB])
            KD = s2("KD", [P, NT, P])
            VT = s2("VT", [P, N3, TH])
            S0 = s2("S0", [P, NB, P])
            SS = s2("SS", [P, PT_TILES, P])
            VM = s2("VM", [P, 2, P])
        PS = ctx.enter_context(nc.psum_tensor("PS", [P, 8, 512], F32))
        PSF = PS[:, :, :].rearrange("p b n -> p (b n)")
        xd = nc.dram_tensor("x_spill", [P, KT * TOK], F32).ap()
        padded = nc.dram_tensor("rel_padded", [AH, 512], F32)
        skewed = nc.dram_tensor("rel_skewed", [P, AH, 512], F32)

        KCA = CACHES[:, 0:4096].rearrange("p (s f n) -> p s f n", s=2, f=AB)
        VCA = CACHES[:, 4096:8192].rearrange("p (s f n) -> p s f n", s=2, f=AB)
        QB = CACHES[:, 8192:9216].rearrange("p (s f n) -> p s f n", s=2, f=AB)
        AT = CACHES[:, 0:AW]
        QT = lambda b: X[:, b, :]
        KTT = lambda b: X[:, AB + b, :]

        def sm(name, i=0, n=1):
            o = SMALL[name][0]
            return small[:, bass.ds(o + i, n)]

        def hh(k, cols):
            return HAH[:, k, cols] if k < AB else HBH[:, k - AB, cols]

        def hl(k, cols):
            return HAL[:, k, cols] if k < AB else HBL[:, k - AB, cols]

        third = lambda n: slice(n * TH, (n + 1) * TH)
        tile = lambda t: slice(t * P, (t + 1) * P)

        s_in = sem("s_in")
        s_small = sem("s_small")
        s_hist = sem("s_hist")
        s_rel = sem("s_rel")
        s_pad = sem("s_pad")
        s_bt = sem("s_bt")
        s_bias = sem("s_bias")
        s_const = sem("s_const")
        s_dc = sem("s_dc")
        s_raw = [sem(f"s_raw{i}") for i in range(3)]
        s_hi = sem("s_hi")
        s_lo = [sem(f"s_lo{i}") for i in range(3)]
        s_sq = sem("s_sq")
        s_ms = sem("s_ms")
        s_rt = sem("s_rt")
        s_dg = sem("s_dg")
        s_rb = sem("s_rb")
        s_hf = sem("s_hf")
        s_hhi = sem("s_hhi")
        s_hlo = sem("s_hlo")
        s_full = {k: sem(f"s_full_{k}") for k in ("g", "a", "q", "k", "v", "vt")}
        s_got = {k: sem(f"s_got_{k}") for k in ("g", "a", "q", "k", "v", "vt")}
        s_cv = sem("s_cv")
        s_co = sem("s_co")
        s_kc = [sem(f"s_kc{i}") for i in range(2)]
        s_vc = [sem(f"s_vc{i}") for i in range(2)]
        s_qb = sem("s_qb")
        s_s = sem("s_s")
        s_nm = sem("s_nm")
        s_p = sem("s_p")
        s_pn = sem("s_pn")
        s_pt = sem("s_pt")
        s_ptc = sem("s_ptc")
        s_o = sem("s_o")
        s_at = sem("s_at")
        s_att = sem("s_att")
        s_ahi = sem("s_ahi")
        s_alo = sem("s_alo")
        s_yc = sem("s_yc")
        s_x = sem("s_x")
        s_xo = sem("s_xo")
        s_xr = [sem(f"s_xr{i}") for i in range(2)]
        s_sp = sem("s_sp")
        s_fa = sem("s_fa")
        s_fb = sem("s_fb")
        s_si = sem("s_si")
        s_u = sem("s_u")
        s_uh = sem("s_uh")
        s_ul = sem("s_ul")
        s_cf = {k: sem(f"s_cf_{k}") for k in "fqvg"}
        s_cg = {k: sem(f"s_cg_{k}") for k in "fqvg"}
        s_vt = sem("s_vt")
        s_vk = sem("s_vk")
        s_lv = sem("s_lv")
        s_mg = sem("s_mg")
        s_up = sem("s_up")
        s_kt = sem("s_kt")
        s_kd = sem("s_kd")
        s_st = sem("s_st")
        s_ss = sem("s_ss")
        s_vm = sem("s_vm")
        s_s0 = sem("s_s0")
        s_sm = sem("s_sm")
        s_sf = sem("s_sf")
        s_sn = sem("s_sn")
        s_oc = sem("s_oc")
        s_oq = sem("s_oq")
        s_og = sem("s_og")
        s_cm = sem("s_cm")
        s_cr = sem("s_cr")
        s_cd = sem("s_cd")
        s_cb = sem("s_cb")
        s_cn = sem("s_cn")
        s_hgp = sem("s_hgp")
        s_hgs = sem("s_hgs")
        s_outc = sem("s_outc")
        s_out = sem("s_out")

        def weights(sp, T, slot, src):
            need(sp, s_lo[slot], T(f"w{slot}"))
            sp.dma_start(WR[:, slot, :], src).then_inc(s_raw[slot], 16)
            T.add(f"w{slot}")

        def ffn_sp(sp, T, layer):
            fi = lambda t: w_fi[t + layer * 2 * FJ, :, :]
            fo = lambda t: w_fo[t + layer * FJ, :, :]

            def w_in(c, slots=(0, 1, 2, 0)):
                for i, slot in enumerate(slots):
                    weights(sp, T, slot, fi(c * 4 + i))

            def w_out(c, slots=(1, 2)):
                for i, slot in enumerate(slots):
                    weights(sp, T, slot, fo(c * 2 + i))
            w_in(0, (0, 1, 2, 1))
            with sp.Fori(0, NCH // 2) as i:
                T.enter(i, w0=4, w1=4, w2=4)
                w_in(2 * i + 1)
                w_out(2 * i)
                w_in(2 * i + 2)
                w_out(2 * i + 1)
                T.leave(NCH // 2)
            w_out(NCH - 1, (0, 1))

        def proj_sp_first(sp, T, w):
            for m in range(2):
                weights(sp, T, m, w[m, :, :])

        def proj_sp(sp, T, w):
            with sp.Fori(0, KT // 2 - 1) as i:
                T.enter(i, w0=1, w1=1)
                for m in range(2):
                    weights(sp, T, m, w[2 * i + 2 + m, :, :])
                T.leave(KT // 2 - 1)

        def sync_program(sp):
            T = Tally()
            sp.dma_start(small[:, :], small_d).then_inc(s_small, 16)
            for n in range(N3):
                sp.dma_start(X[:, :, third(n)], x_t.rearrange("p (k t) -> p k t", k=KT)[:, :, third(n)]).then_inc(s_in, 16)
                sp.wait_ge(s_in, 16 * (n + 1))
            sp.dma_start(US[:, :, :, 0:HIST], hist_d).then_inc(s_hist, 16)

            def ab(j):
                for slot, m in ((0, 16), (1, 12), (2, 0), (0, 4), (1, 8)):
                    weights(sp, T, slot, w_ab[j + m, :, :])
            sp.wait_ge(s_const, N_CONST)
            sp.wait_ge(s_rel, 32)
            ab(0)
            with sp.Fori(0, AB - 1) as i:
                T.enter(i, w0=2, w1=2, w2=1)
                ab(i + 1)
                T.leave(AB - 1)
            proj_sp_first(sp, T, w_oab)
            sp.wait_ge(s_full["v"], N3 * AB)
            for b in range(NB):
                if b >= 2:
                    sp.wait_ge(s_s, b - 1)
                sp.dma_start(KCA[:, b % 2], kc_d[b]).then_inc(s_kc[b % 2], 16)
                if b >= 2:
                    sp.wait_ge(s_o, b - 1)
                sp.dma_start(VCA[:, b % 2], vc_d[b]).then_inc(s_vc[b % 2], 16)
            sp.wait_ge(s_got["k"], N3 * AB)
            sp.dma_start(k_o, X[:, AB:KT, SEQ - CACHE:TOK]).then_inc(s_out, 16)
            sp.wait_ge(s_got["vt"], N3 * AB)
            sp.dma_start(v_o, VTOK[:, 4:NT, :]).then_inc(s_out, 16)
            sp.wait_ge(s_s, NB + AH * PT_TILES)
            sp.wait_ge(s_out, 32)
            sp.wait_ge(s_outc, 32)
            xv = x_t.rearrange("p (k t) -> p k t", k=KT)
            sp.dma_start(X[:, 0:2, :], xv[:, 0:2, :]).then_inc(s_xr[0], 16)
            sp.dma_start(X[:, 2:KT, :], xv[:, 2:KT, :]).then_inc(s_xr[1], 16)
            proj_sp(sp, T, w_oab)
            ffn_sp(sp, T, 0)
            sp.wait_ge(s_x, XC_START)
            sp.dma_start(xd, X[:, :, :].rearrange("p k t -> p (k t)")).then_inc(s_sp, 16)

            def head(h):
                for slot, m in ((0, 8), (1, 0), (2, 16), (1, 24)):
                    weights(sp, T, slot, w_c[h + m, :, :])
            head(0)
            head(1)
            with sp.Fori(0, CH // 2 - 1) as i:
                T.enter(i, w0=2, w1=4, w2=2)
                head(2 * i + 2)
                head(2 * i + 3)
                T.leave(CH // 2 - 1)
            proj_sp_first(sp, T, w_oc)
            sp.wait_ge(s_hlo, H_CO)
            xdv = xd.rearrange("p (k t) -> p k t", k=KT)
            sp.dma_start(X[:, 0:2, :], xdv[:, 0:2, :]).then_inc(s_xr[0], 16)
            sp.dma_start(X[:, 2:KT, :], xdv[:, 2:KT, :]).then_inc(s_xr[1], 16)
            proj_sp(sp, T, w_oc)
            ffn_sp(sp, T, 1)
            yv = y_o.rearrange("p (k t) -> p k t", k=KT)
            for n in range(N3):
                sp.wait_ge(s_hf, HF_END - N3 + n + 1)
                sp.dma_start(yv[:, :, third(n)], X[:, :, third(n)]).then_inc(s_out, 16)
            sp.wait_ge(s_out, 16 * (2 + N3))
            sp.wait_ge(s_hgp, 16 * CH)
            sp.wait_ge(s_hgs, 16 * CH)

        N_CONST = 4 + 5 * LEVELS
        X_AB = N3 * KT
        XC_START = X_AB + NCH * KT * N3
        X_C = XC_START + N3 * KT
        X_END = X_C + NCH * KT * N3
        H_AB = 2 * N3
        H_ABO = H_AB + N3
        H_F0 = H_ABO + 2 * N3
        H_C = H_F0 + 2 * N3
        H_CO = H_C + 2 * N3
        H_F1 = H_CO + 2 * N3
        HF_END = 6 * N3

        def pool_program(pool):
            rel = WR[0:AH, 1, 0:P + 257]
            pool.dma_start(rel[:, P:], rel_d).then_inc(s_rel, 16)
            pool.wait_ge(s_rel, 16)
            pool.tensor_copy(rel[:, 0:P], rel[:, P:P + 1].to_broadcast([AH, P])).then_inc(s_pad, 1)
            pool.wait_ge(s_pad, 1)
            pool.dma_start(padded.ap()[:, 0:P + 257], rel).then_inc(s_rel, 16)
            pool.wait_ge(s_rel, 32)
            pool.dma_start(skewed.ap()[:, :, 0:P + 257],
                           bass.AP(tensor=padded, offset=0, ap=[[0, P], [512, AH], [1, P + 257]])).then_inc(s_rel, 16)
            pool.memset(ident[:, :], 0.0).then_inc(s_const, 1)
            pool.memset(ones[:, :], 1.0).then_inc(s_const, 1)
            pool.wait_ge(s_const, 2)
            pool.affine_select(out=ident[:, :], in_=ident[:, :], compare_op=ALU.not_equal, fill=1.0,
                               base=0, pattern=[[-1, P]], channel_multiplier=1).then_inc(s_const, 1)
            pool.iota(parity_i[:, 0:1], pattern=[[0, 1]], base=0, channel_multiplier=1).then_inc(s_const, 1)
            mf = WR[:, 2, 0:P]
            n = 4
            for lv in range(LEVELS):
                w = 1 << lv
                nb = P // (2 * w)
                pool.memset(mf, 0.0).then_inc(s_const, 1)
                n += 1
                pool.wait_ge(s_const, n)
                right = mf.rearrange("p (b two w) -> p b two w", two=2, w=w)[:, :, 1, :]
                pool.memset(right, 1.0).then_inc(s_const, 1)
                n += 1
                pool.wait_ge(s_const, n)
                for base, st, cm in ((0, -2 * w, 1), (w - 1, 2 * w, -1)):
                    pool.affine_select(out=right, in_=right, compare_op=ALU.is_ge, fill=0.0, base=base,
                                       pattern=[[st, nb], [0, w]], channel_multiplier=cm).then_inc(s_const, 1)
                    n += 1
                    pool.wait_ge(s_const, n)
                pool.tensor_copy(lvl_mask[:, lv, :], mf).then_inc(s_const, 1)
                n += 1
                pool.wait_ge(s_const, n)
            pool.wait_ge(s_rel, 48)
            pool.wait_ge(s_cv, 2 * CW * AB)
            pool.wait_ge(s_co, AB)
            pool.dma_start(cvp_o, CO[:, :, :]).then_inc(s_outc, 16)
            pool.dma_start(cvs_o, US[:, :, :, NS:HIST + NS]).then_inc(s_outc, 16)
            pool.wait_ge(s_outc, 32)
            pool.wait_ge(s_full["vt"], N3 * AB)
            pitch = AH * 512 - 1
            pool.dma_start(BT[:, :, :], bass.AP(tensor=skewed, offset=P, ap=[[pitch, P], [512, AH], [1, 2 * P]])).then_inc(s_bt, 16)
            for h in range(AH):
                pool.dma_start(BS[h * NS:(h + 1) * NS, :],
                               bass.AP(tensor=skewed, offset=P + 512 * h, ap=[[pitch, NS], [1, P + NS]])).then_inc(s_bt, 16)

        def cut_hi(act, T, slot, after=None):
            T.add(f"w{slot}")
            need(act, s_raw[slot], T(f"w{slot}") * 16)
            if after is not None:
                need(act, *after)
            act.activation(WH[:, slot, :], WR[:, slot, :], ACT.Copy).then_inc(s_hi, 1)

        def cut_lo(dve, T, slot):
            T.add("hi")
            need(dve, s_hi, T("hi"))
            dve.tensor_tensor(WL[:, slot, :], WR[:, slot, :], WH[:, slot, :].bitcast(F32),
                              ALU.subtract).then_inc(s_lo[slot], 1)

        def have(pe, T, slot):
            T.add(f"w{slot}")
            need(pe, s_lo[slot], T(f"w{slot}"))

        def product(out, slot, n):
            mm = None
            for k in range(KT):
                wh, wl = WH[:, slot, tile(k)], WL[:, slot, tile(k)]
                nc.tensor.matmul(out, wh, hh(k, third(n)), start=(k == 0), stop=False)
                nc.tensor.matmul(out, wh, hl(k, third(n)), start=False, stop=False)
                mm = nc.tensor.matmul(out, wl, hh(k, third(n)), start=False, stop=(k == KT - 1))
            return mm

        def norm_act(act, T, x_count, final=False):
            def a(n):
                need(act, s_x, x_count)
                if x_count == 0:
                    act.wait_ge(s_in, 16 * (n + 1))
                need(act, s_ms, T("ms"))
                for half in range(2):
                    ks = slice(half * AB, (half + 1) * AB)
                    act.activation(SQ[:, ks, :], X[:, ks, third(n)], ACT.Square).then_inc(s_sq, 1)
                T.add("ms")
                act.wait_ge(s_ms, T("ms"))
                act.activation(rt[:, 3 * n:3 * n + 3], PS[:, 7, 3 * n:3 * n + 3], ACT.Sqrt,
                               bias=eps[:, 0:1], scale=1.0 / D).then_inc(s_rt, 1)

            def b(n):
                T.add("hf")
                act.wait_ge(s_hf, T("hf"))
                act.activation(HAH[:, :, third(n)], HF[:, 0:AB, :], ACT.Copy).then_inc(s_hhi, 1)
                act.activation(HBH[:, :, third(n)], HF[:, AB:KT, :], ACT.Copy).then_inc(s_hhi, 1)
            a(0)
            a(1)
            if not final:
                b(0)
            a(2)
            if final:
                T.add("hf", N3)
            else:
                b(1)
                b(2)

        def norm_pe(pe, T):
            for n in range(N3):
                T.add("sq", 2)
                pe.wait_ge(s_sq, T("sq"))
                for tt in range(TPT):
                    for k in range(KT):
                        mm = nc.tensor.matmul(PS[:, 7, 3 * n + tt:3 * n + tt + 1], SQ[:, k, tile(tt)], ones[:, 0:1],
                                              start=(k == 0), stop=(k == KT - 1))
                mm.then_inc(s_ms, 1)
                T.add("dg")
                pe.wait_ge(s_dg, T("dg"))
                nc.tensor.matmul(PS[:, 4 + n, 0:TH], ones[:, :], DG[:, :, :].rearrange("p a b -> p (a b)"),
                                 start=True, stop=True).then_inc(s_rb, 1)

        def norm_dve(dve, T, gain, final=False):
            def a(n):
                T.add("rt")
                dve.wait_ge(s_rt, T("rt"))
                if n:
                    dve.wait_ge(s_rb, T("rb_made"))
                T.add("rb_made")
                link(dve, T, dve.reciprocal(ri[:, 3 * n:3 * n + 3], rt[:, 3 * n:3 * n + 3]))
                dve.tensor_tensor(DG[:, :, :], ident[:, :].unsqueeze(1).to_broadcast([P, TPT, P]),
                                  ri[:, 3 * n:3 * n + 3].unsqueeze(2).to_broadcast([P, TPT, P]),
                                  ALU.mult).then_inc(s_dg, 1)

            def b(n):
                T.add("rb")
                dve.wait_ge(s_rb, T("rb"))
                if not final:
                    need(dve, s_hhi, T("hhi"))
                    need(dve, s_hlo, T("hlo"))
                for k in range(KT):
                    out = X[:, k, third(n)] if final else HF[:, k, :]
                    ins = dve.scalar_tensor_tensor(out=out, in0=X[:, k, third(n)], scalar=sm("gain", gain * KT + k),
                                                   in1=PS[:, 4 + n, 0:TH], op0=ALU.mult, op1=ALU.mult)
                ins.then_inc(s_hf, 1)
                if final:
                    return
                for half, hi, lo in ((0, HAH, HAL), (1, HBH, HBL)):
                    T.add("hhi")
                    dve.wait_ge(s_hhi, T("hhi"))
                    dve.tensor_tensor(lo[:, :, third(n)], HF[:, half * AB:(half + 1) * AB, :],
                                      hi[:, :, third(n)].bitcast(F32), ALU.subtract).then_inc(s_hlo, 1)
                    T.add("hlo")
            a(0)
            a(1)
            b(0)
            a(2)
            b(1)
            b(2)

        def link(dve, T, ins):
            T.add("dc")
            ins.then_inc(s_dc, 1)
            dve.wait_ge(s_dc, T("dc"))

        def proj_pe(pe, T, ready):
            def block(m, first):
                slot = m
                have(pe, T, slot)
                for n in range(N3):
                    if first and m == 0:
                        ready(n)
                    if not first:
                        need(pe, s_x, T("x") - 2 * N3 + 1)
                    T.add("x")
                    product(PS[:, 3 * m + n, 0:TH], slot, n).then_inc(s_xo, 1)
            block(0, True)
            block(1, True)
            with pe.Fori(0, KT // 2 - 1) as i:
                T.enter(i, w0=1, w1=1, x=2 * N3)
                block(0, False)
                block(1, False)
                T.leave(KT // 2 - 1)

        def proj_act(act, T):
            def block(m, first):
                cut_hi(act, T, 1 - m, None if first and m == 0 else (s_xo, T("x")))
                T.add("x", N3)
            block(0, True)
            block(1, True)
            with act.Fori(0, KT // 2 - 1) as i:
                T.enter(i, w0=1, w1=1, x=2 * N3)
                block(0, False)
                block(1, False)
                T.leave(KT // 2 - 1)

        def proj_dve(dve, T, reloaded):
            def block(m, blk, first):
                cut_lo(dve, T, 1 - m)
                if first and m == 0:
                    dve.wait_ge(s_xr[0], 16 * reloaded)
                if not first:
                    pass
                for n in range(N3):
                    T.add("x")
                    need(dve, s_xo, T("x"))
                    xs = X[:, blk, third(n)]
                    dve.tensor_tensor(xs, xs, PS[:, 3 * m + n, 0:TH], ALU.add).then_inc(s_x, 1)
            block(0, 0, True)
            block(1, 1, True)
            dve.wait_ge(s_xr[1], 16 * reloaded)
            with dve.Fori(0, KT // 2 - 1) as i:
                T.enter(i, x=2 * N3, hi=2)
                block(0, i * 2 + 2, False)
                block(1, i * 2 + 3, False)
                T.leave(KT // 2 - 1)

        def ffn_pe(pe, T, ready):
            def w_in(first):
                sa, sb_ = ((0, 2), (1, 1)) if first else ((0, 2), (1, 0))
                for j in range(2):
                    have(pe, T, sa[j])
                    for n in range(N3):
                        if first and j == 0:
                            ready(n)
                        need(pe, s_si, T("fj") - 2)
                        T.add("fj")
                        product(PS[:, n, 0:TH], sa[j], n).then_inc(s_fa, 1)
                    have(pe, T, sb_[j])
                    for n in range(N3):
                        need(pe, s_u, T("fb") - 2)
                        T.add("fb")
                        product(PS[:, 3 + n, 0:TH], sb_[j], n).then_inc(s_fb, 1)

            def w_out(par, slots=(1, 2)):
                for slot in slots:
                    have(pe, T, slot)
                T.add("u", 2 * N3)
                need(pe, s_ul, T("u"))
                for m in range(KT):
                    for n in range(N3):
                        i = m * N3 + n
                        out = PS[:, 6 + i % 2, 0:TH]
                        need(pe, s_x, T("x") - 1)
                        T.add("x")
                        for kk in range(2):
                            wh, wl = WH[:, slots[kk], tile(m)], WL[:, slots[kk], tile(m)]
                            uh, ul = UH[:, par, kk, third(n)], UL[:, par, kk, third(n)]
                            nc.tensor.matmul(out, wh, uh, start=(kk == 0), stop=False)
                            nc.tensor.matmul(out, wh, ul, start=False, stop=False)
                            mm = nc.tensor.matmul(out, wl, uh, start=False, stop=(kk == 1))
                        mm.then_inc(s_xo, 1)
            w_in(True)
            with pe.Fori(0, NCH // 2) as i:
                T.enter(i, w0=4, w1=4, w2=4, fj=4 * N3, fb=4 * N3, u=4 * N3, x=2 * KT * N3)
                w_in(False)
                w_out(0)
                w_in(False)
                w_out(1)
                T.leave(NCH // 2)
            w_out(0, (0, 1))

        def ffn_act(act, T):
            def w_in(par, first=False):
                for j in range(2):
                    if j == 0:
                        cut_hi(act, T, 1, (s_xo, T("x")))
                    elif first:
                        cut_hi(act, T, 1, (s_fb, T("u")))
                    else:
                        cut_hi(act, T, 0, (s_fa, T("fj")))
                    for n in range(N3):
                        T.add("fj")
                        need(act, s_fa, T("fj"))
                        need(act, s_u, T("fj") - N3)
                        act.activation(SG[:, n, :], PS[:, n, 0:TH], ACT.Silu).then_inc(s_si, 1)
                    if j == 0:
                        cut_hi(act, T, 2, (s_xo, T("x")))
                    elif first:
                        cut_hi(act, T, 0, (s_fa, T("fj")))
                    else:
                        cut_hi(act, T, 1, (s_fb, T("u")))
                        cut_hi(act, T, 2, (s_fa, T("fj")))
                    for n in range(N3):
                        T.add("u")
                        need(act, s_u, T("u"))
                        need(act, s_xo, T("x"))
                        act.activation(UH[:, par, j, third(n)], UF[:, n, :], ACT.Copy).then_inc(s_uh, 1)

            def w_out():
                cut_hi(act, T, 0, (s_fb, T("u")))
                T.add("x", KT * N3)
            w_in(0, True)
            with act.Fori(0, NCH // 2) as i:
                T.enter(i, w0=4, w1=4, w2=4, fj=4 * N3, u=4 * N3, x=2 * KT * N3)
                w_in(1)
                w_out()
                w_in(0)
                w_out()
                T.leave(NCH // 2)
            cut_hi(act, T, 1, (s_xo, T("x")))
            T.add("x", KT * N3)

        def ffn_dve(dve, T):
            def w_in(par, first=False):
                for j in range(2):
                    cut_lo(dve, T, 1 if j == 0 or first else 0)
                    if j == 0:
                        cut_lo(dve, T, 2)
                    elif first:
                        cut_lo(dve, T, 0)
                    else:
                        cut_lo(dve, T, 1)
                        cut_lo(dve, T, 2)
                    for n in range(N3):
                        T.add("u")
                        need(dve, s_si, T("u"))
                        need(dve, s_fb, T("u"))
                        need(dve, s_uh, T("u") - N3)
                        need(dve, s_ul, T("u") - N3)
                        dve.tensor_tensor(UF[:, n, :], SG[:, n, :], PS[:, 3 + n, 0:TH], ALU.mult).then_inc(s_u, 1)
                        if n:
                            lo(par, j, n - 1, T("u") - 1)
                    lo(par, j, N3 - 1, T("u"))

            def lo(par, j, n, count):
                need(dve, s_uh, count)
                dve.tensor_tensor(UL[:, par, j, third(n)], UF[:, n, :],
                                  UH[:, par, j, third(n)].bitcast(F32), ALU.subtract).then_inc(s_ul, 1)

            def w_out(slot=0):
                cut_lo(dve, T, slot)
                for m in range(KT):
                    for n in range(N3):
                        i = m * N3 + n
                        T.add("x")
                        need(dve, s_xo, T("x"))
                        xs = X[:, m, third(n)]
                        dve.tensor_tensor(xs, xs, PS[:, 6 + i % 2, 0:TH], ALU.add).then_inc(s_x, 1)
            w_in(0, True)
            with dve.Fori(0, NCH // 2) as i:
                T.enter(i, hi=12, u=4 * N3, x=2 * KT * N3)
                w_in(1)
                w_out()
                w_in(0)
                w_out()
                T.leave(NCH // 2)
            w_out(1)

        def ab_pe(pe, T):
            def step(ready=None):
                for name, slot, bank, prev, sem_prev in (
                        ("g", 0, 0, "v", s_got["v"]), ("a", 1, 3, "k", s_got["k"]), ("q", 2, 0, "g", s_got["g"]),
                        ("k", 0, 3, "a", s_got["a"]), ("v", 1, 0, "q", s_got["q"])):
                    have(pe, T, slot)
                    for n in range(N3):
                        if ready and name == "g":
                            ready(n)
                        need(pe, sem_prev, T(prev) - 2 + n)
                        product(PS[:, bank + n, 0:TH], slot, n).then_inc(s_full[name], 1)
                        if name == "v" and n:
                            turn(n - 1)
                    T.add(name, N3)
                turn(N3 - 1)
                T.add("vt", N3)

            def turn(n):
                j3 = T("vt")
                need(pe, s_got["v"], j3 + n + 1)
                need(pe, s_got["vt"], j3 + (0, -1, 1)[n])
                for tt in range(TPT):
                    mm = nc.tensor.transpose(PS[:, 6 + n % 2, tile(tt)], EV[:, n, tile(tt)], ident[:, :])
                mm.then_inc(s_full["vt"], 1)
            step(lambda n: pe.wait_ge(s_hlo, 2 * (n + 1)))
            with pe.Fori(0, AB - 1) as i:
                T.enter(i, w0=2, w1=2, w2=1, g=N3, a=N3, q=N3, k=N3, v=N3, vt=N3)
                step()
                T.leave(AB - 1)

        def ab_act(act, T):
            def step(j, first):
                three = T("j3")
                wait = lambda k: None if first else (s_full[k], three)
                here = lambda k: (s_full[k], three + N3)
                cut_hi(act, T, 1, wait("v"))
                for n in range(N3):
                    need(act, s_full["g"], three + n + 1)
                    need(act, s_full["vt"], three - 2 + n)
                    act.activation(EV[:, n, :], PS[:, n, 0:TH], ACT.Sigmoid).then_inc(s_got["g"], 1)
                cut_hi(act, T, 2, wait("q"))
                cut_hi(act, T, 0, here("g"))
                for n in range(N3):
                    need(act, s_full["q"], three + n + 1)
                    act.activation(X[:, j, third(n)], PS[:, n, 0:TH], ACT.Copy, scale=AD ** -0.5).then_inc(s_got["q"], 1)
                cut_hi(act, T, 1, here("a"))
                for n in range(N3):
                    need(act, s_full["k"], three + n + 1)
                    act.activation(X[:, j + AB, third(n)], PS[:, 3 + n, 0:TH], ACT.Copy).then_inc(s_got["k"], 1)
                cut_hi(act, T, 0, here("k"))
                for n in range(N3):
                    need(act, s_full["v"], three + n + 1)
                    need(act, s_got["a"], three + n + 1)
                    act.activation(EV[:, n, :], PS[:, n, 0:TH], ACT.Copy).then_inc(s_got["v"], 1)
                T.add("j3", N3)
            step(0, True)
            with act.Fori(0, AB - 1) as i:
                T.enter(i, w0=2, w1=2, w2=1, j3=N3)
                step(i + 1, False)
                T.leave(AB - 1)

        def ab_dve(dve, T):
            def conv(j, a, b):
                for t in range(a, b):
                    for part in range(2):
                        if part == 0:
                            src, out = UP[:, t:t + SEQ], Y[:, j, 0:SEQ]
                        else:
                            src = US[:, j, :, t:t + NS]
                            out = Y[:, j, SEQ:TOK].rearrange("p (b s) -> p b s", b=NB)
                        w = sm("cw", j * CW + t)
                        if t == 0:
                            ins = dve.tensor_scalar(out, src, w, sm("cb", j), ALU.mult, ALU.add)
                        else:
                            need(dve, s_cv, T("cv") - 1)
                            ins = dve.scalar_tensor_tensor(out=out, in0=src, scalar=w, in1=out, op0=ALU.mult, op1=ALU.add)
                        ins.then_inc(s_cv, 1)
                        T.add("cv")

            def step(j):
                three = T("j3")
                cut_lo(dve, T, 1)
                cut_lo(dve, T, 2)
                need(dve, s_co, T("co"))
                need(dve, s_cv, T("cv"))
                for n in range(N3):
                    need(dve, s_full["a"], three + n + 1)
                    need(dve, s_got["g"], three + n + 1)
                    w = TH if n < N3 - 1 else SEQ - (N3 - 1) * TH
                    ins = dve.tensor_tensor(UP[:, HIST + n * TH:HIST + n * TH + w], EV[:, n, 0:w], PS[:, 3 + n, 0:w], ALU.mult)
                    if n == N3 - 1:
                        bs = lambda ap: ap.rearrange("p (b s) -> p b s", b=NB)
                        ins = dve.tensor_tensor(US[:, j, :, HIST:HIST + NS], bs(EV[:, n, w:TH]), bs(PS[:, 3 + n, w:TH]), ALU.mult)
                    ins.then_inc(s_got["a"], 1)
                need(dve, s_got["a"], three + N3)
                dve.tensor_copy(CO[:, j, :], UP[:, SEQ:SEQ + HIST]).then_inc(s_co, 1)
                T.add("co")
                conv(j, 0, 5)
                cut_lo(dve, T, 0)
                conv(j, 5, 14)
                cut_lo(dve, T, 1)
                conv(j, 14, 22)
                cut_lo(dve, T, 0)
                for n in range(N3):
                    need(dve, s_full["vt"], three + n + 1)
                    dve.tensor_copy(VTOK[:, 3 * n:3 * n + 3, bass.ds(j * P, P)],
                                    PS[:, 6 + n % 2, 0:TH].rearrange("p (a b) -> p a b", b=P)).then_inc(s_got["vt"], 1)
                    conv(j, 22 + 3 * n, 25 + 3 * n)
                T.add("j3", N3)
            dve.memset(UP[:, 0:HIST], 0.0).then_inc(s_dc, 1)
            T.add("dc")
            dve.wait_ge(s_dc, T("dc"))
            dve.wait_ge(s_hist, 16)
            step(0)
            with dve.Fori(0, AB - 1) as i:
                T.enter(i, hi=5, j3=N3, co=1, cv=2 * CW)
                step(i + 1)
                T.leave(AB - 1)

        ITEMS = NB + PT_TILES * AH

        def item(s):
            t, h = divmod(s - NB, AH)
            return t, h, min(t + 1, 5)

        def score(s, cols):
            o = (s % 2) * 1024
            return PSF[:, o + cols.start:o + cols.stop]

        def att_pe(pe, T):
            def scores(s):
                if s >= 2:
                    pe.wait_ge(s_p, s - 1)
                if s < NB:
                    pe.wait_ge(s_kc[s % 2], 16 * (s // 2 + 1))
                    pe.wait_ge(s_qb, s + 1)
                    for f in range(AB):
                        nc.tensor.matmul(score(s, slice(0, CACHE)), QB[:, s % 2, f, :], KCA[:, s % 2, f, :],
                                         start=(f == 0), stop=(f == AB - 1))
                    for f in range(AB):
                        mm = nc.tensor.matmul(score(s, slice(CACHE, CACHE + NS)), QB[:, s % 2, f, :],
                                              X[:, AB + f, SEQ + NS * s:SEQ + NS * (s + 1)],
                                              start=(f == 0), stop=(f == AB - 1))
                    mm.then_inc(s_s, 1)
                    return
                t, h, nk = item(s)
                r = slice(64 * (h % 2), 64 * (h % 2) + 64)
                q = X[r, h // 2, tile(t)]
                for lo, hi in ((5 - nk, min(4, 5)), (4, 5)):
                    if lo == hi:
                        continue
                    k0 = (t - 4 + lo) * P
                    cols = slice(lo * P, hi * P)
                    kk = X[r, AB + h // 2, k0:k0 + (hi - lo) * P]
                    cut = nk == 5 and lo == 0
                    mm = nc.tensor.matmul(score(s, cols), q, kk, start=True, stop=True)
                    if cut:
                        mm = nc.tensor.matmul(score(s, slice(0, 64)), late[:, :], minus[:, :], start=False, stop=True,
                                              skip_group_check=True)
                mm.then_inc(s_s, 1)

            def turn(s):
                if s < NB:
                    pe.wait_ge(s_pn, s + 1)
                    tiles = range(5)
                else:
                    pe.wait_ge(s_p, s + 1)
                    tiles = range(5 - item(s)[2], 5)
                need(pe, s_ptc, s)
                if s > NB:
                    pe.wait_ge(s_alo, 4 + T("att"))
                for c in tiles:
                    mm = nc.tensor.transpose(PSF[:, 2048 + c * P:2048 + (c + 1) * P], PR[:, s % 2, tile(c)], ident[:, :])
                mm.then_inc(s_pt, 1)

            def values(s):
                pe.wait_ge(s_ptc, s + 1)
                if s < NB:
                    pe.wait_ge(s_vc[s % 2], 16 * (s // 2 + 1))
                    for f in range(AB):
                        out = PS[:, 6 + f // 2, (f % 2) * 256 + s * 32:(f % 2) * 256 + s * 32 + 32]
                        for c in range(5):
                            v = VCA[:, s % 2, c, tile(f)] if c < 4 else VTOK[:, NT - 1, tile(f)]
                            mm = nc.tensor.matmul(out, v, PRT[:, s % 2, c * P + 32 * f:c * P + 32 * f + 32],
                                                  start=(c == 0), stop=(c == 4))
                    mm.then_inc(s_o, 1)
                    return
                t, h, nk = item(s)
                if h == 0:
                    if t < 2:
                        pe.wait_ge(s_alo, 4)
                    else:
                        pe.wait_ge(s_at, t - 1)
                for c in range(5 - nk, 5):
                    mm = nc.tensor.matmul(PS[:, 6 + t % 2, h * AD:(h + 1) * AD], PRT[:, s % 2, tile(c)],
                                          VTOK[:, t - 4 + c, h * AD:(h + 1) * AD], start=(c == 5 - nk), stop=(c == 4))
                mm.then_inc(s_o, 1)

            def back(t):
                pe.wait_ge(s_at, t + 1)
                pe.wait_ge(s_ptc, min(NB + AH * (t + 1) + 2, ITEMS))
                for f in range(AB):
                    mm = nc.tensor.transpose(PS[:, 4, tile(f)], AT[:, tile(f)], ident[:, :])
                mm.then_inc(s_att, 1)
                T.add("att")

            pe.wait_ge(s_got["k"], N3 * AB)
            pe.wait_ge(s_got["q"], N3 * AB)
            pe.wait_ge(s_got["vt"], N3 * AB)
            pe.wait_ge(s_got["a"], N3 * AB)
            scores(0)
            for s in range(ITEMS + 1):
                if s + 1 < ITEMS:
                    scores(s + 1)
                if s >= NB + AH + 2 and (s - 2) % AH == 0:
                    back((s - 2 - NB) // AH - 1)
                if s < ITEMS:
                    turn(s)
                if s:
                    values(s - 1)
            back(PT_TILES - 1)

        def att_act(act, T):
            def probs(s):
                act.wait_ge(s_nm, s + 1)
                if s >= 2:
                    act.wait_ge(s_pt, s - 1)
                if s < NB:
                    act.activation(PR[:, s % 2, 0:CACHE], score(s, slice(0, CACHE)), ACT.Exp, bias=nmax[:, s % 2:s % 2 + 1],
                                   accum_out=psum_[:, 0 + 2 * (s % 2):1 + 2 * (s % 2)])
                    act.activation(PR[:, s % 2, CACHE + NS * s:CACHE + NS * (s + 1)], score(s, slice(CACHE, CACHE + NS)), ACT.Exp,
                                   bias=nmax[:, s % 2:s % 2 + 1],
                                   accum_out=psum_[:, 1 + 2 * (s % 2):2 + 2 * (s % 2)]).then_inc(s_p, 1)
                    return
                t, h, nk = item(s)
                cols = slice((5 - nk) * P, 5 * P)
                if h == 0 and t >= 2:
                    act.wait_ge(s_at, t - 1)
                act.activation(PR[:, s % 2, cols], score(s, cols), ACT.Exp, bias=nmax[:, s % 2:s % 2 + 1],
                               accum_out=sums[:, t % 2, h:h + 1]).then_inc(s_p, 1)

            def turned(s):
                act.wait_ge(s_pt, s + 1)
                if s >= 2:
                    act.wait_ge(s_o, s - 1)
                nk = 5 if s < NB else item(s)[2]
                cols = slice((5 - nk) * P, 5 * P)
                act.activation(PRT[:, s % 2, cols], PSF[:, 2048 + cols.start:2048 + cols.stop], ACT.Copy).then_inc(s_ptc, 1)

            def sample_hi():
                act.wait_ge(s_o, NB)
                for f2 in range(2):
                    for half in range(2):
                        r = slice(64 * half, 64 * half + 64)
                        act.activation(HAH[r, 2 * f2:2 * f2 + 2, SEQ:TOK].rearrange("p f (b i) -> p f b i", b=NB),
                                       sample_out(f2, half), ACT.Copy).then_inc(s_ahi, 1)

            def back(t):
                act.wait_ge(s_att, t + 1)
                act.activation(HAH[:, :, tile(t)], PS[:, 4, :].rearrange("p (f n) -> p f n", f=AB), ACT.Copy).then_inc(s_ahi, 1)
            for s in range(ITEMS + 1):
                if s < ITEMS:
                    probs(s)
                if 1 <= s <= ITEMS:
                    turned(s - 1)
                if s == NB + 1:
                    sample_hi()
                if s >= NB + AH + 2 and (s - 2) % AH == 0:
                    back((s - 2 - NB) // AH - 1)
            back(PT_TILES - 1)

        def sample_out(f2, half):
            return PS[64 * half:64 * half + 64, 6 + f2, :].rearrange(
                "p (f b two i) -> p f b two i", f=2, b=NB, two=2)[:, :, :, half, :]

        def att_dve(dve, T):
            dve.wait_ge(s_bt, 16 * (1 + AH))
            dve.tensor_copy(rt[:, 8:9], BS[:, 0:1])
            link(dve, T, dve.tensor_copy(rt[:, 0:AH], BT[:, :, 0]))
            link(dve, T, dve.tensor_tensor(BT[:, :, :], BT[:, :, :], rt[:, 0:AH].unsqueeze(2).to_broadcast([P, AH, 2 * P]),
                                           ALU.subtract))
            dve.tensor_scalar(BT[0:64, :, P + 64:2 * P], BT[0:64, :, P + 64:2 * P], NEG, None, ALU.add).then_inc(s_bias, 1)
            dve.tensor_scalar(BS[:, :], BS[:, :], rt[:, 8:9], None, ALU.subtract).then_inc(s_bias, 1)
            for b in range(2):
                dve.memset(QB[:, b, :, :], 0.0).then_inc(s_bias, 1)
                dve.memset(PR[:, b, CACHE:5 * P], 0.0).then_inc(s_bias, 1)
            dve.memset(late[:, :], 0.0).then_inc(s_bias, 1)
            dve.memset(minus[:, :], NEG).then_inc(s_bias, 1)
            dve.wait_ge(s_bias, 8)
            dve.memset(late[:, 64:P], 1.0).then_inc(s_bias, 1)
            dve.wait_ge(s_bias, 9)

            def queries(s):
                if s >= 2:
                    dve.wait_ge(s_s, s - 1)
                for half in range(2):
                    r = slice(64 * half, 64 * half + 64)
                    out = CACHES[r, 8192 + (s % 2) * 512 + half * NS:8192 + (s % 2) * 512 + half * NS + 3 * (P + 2 * NS) + NS]
                    out = bass.AP(tensor=out.tensor, offset=out.offset,
                                  ap=[list(out.ap[0]), [P + 2 * NS, AB], [1, NS]])
                    ins = dve.tensor_copy(out, X[r, 0:AB, SEQ + NS * s:SEQ + NS * (s + 1)])
                ins.then_inc(s_qb, 1)

            def maximum(s):
                dve.wait_ge(s_s, s + 1)
                if s >= 2:
                    dve.wait_ge(s_p, s - 1)
                    dve.wait_ge(s_nm, s - 1)
                if s < NB:
                    near, table, cols = slice(CACHE - P, CACHE + NS), BS[:, :], slice(0, CACHE + NS)
                else:
                    t, h, nk = item(s)
                    nn = min(nk, 2)
                    near, table = slice((5 - nn) * P, 5 * P), BT[:, h, (2 - nn) * P:2 * P]
                    cols = slice((5 - nk) * P, 5 * P)
                link(dve, T, dve.tensor_tensor(score(s, near), score(s, near), table, ALU.add))
                link(dve, T, dve.tensor_reduce(rmax[:, s % 2:s % 2 + 1], score(s, cols), AX.X, ALU.max))
                dve.tensor_scalar(nmax[:, s % 2:s % 2 + 1], rmax[:, s % 2:s % 2 + 1], -1.0, None, ALU.mult).then_inc(s_nm, 1)

            def normalise(s):
                o = 2 * (s % 2)
                dve.wait_ge(s_p, s + 1)
                need(dve, s_pn, s)
                if s >= 2:
                    link(dve, T, dve.memset(PR[:, s % 2, CACHE + NS * (s - 2):CACHE + NS * (s - 1)], 0.0))
                link(dve, T, dve.tensor_tensor(rsum[:, 0:1], psum_[:, o:o + 1], psum_[:, o + 1:o + 2], ALU.add))
                link(dve, T, dve.reciprocal(rsum[:, 1:2], rsum[:, 0:1]))
                dve.tensor_scalar(PR[:, s % 2, :], PR[:, s % 2, :], rsum[:, 1:2], None, ALU.mult).then_inc(s_pn, 1)

            def rows(t):
                dve.wait_ge(s_o, NB + AH * (t + 1))
                if t:
                    dve.wait_ge(s_att, t)
                    dve.wait_ge(s_at, t)
                link(dve, T, dve.reciprocal(rsums[:, :], sums[:, t % 2, :]))
                dve.tensor_tensor(AT.rearrange("p (h d) -> p h d", h=AH), PS[:, 6 + t % 2, :].rearrange("p (h d) -> p h d", h=AH),
                                  rsums[:, :].unsqueeze(2).to_broadcast([P, AH, AD]), ALU.mult).then_inc(s_at, 1)

            def back(t):
                dve.wait_ge(s_ahi, 4 + t + 1)
                dve.tensor_tensor(HAL[:, :, tile(t)], PS[:, 4, :].rearrange("p (f n) -> p f n", f=AB),
                                  HAH[:, :, tile(t)].bitcast(F32), ALU.subtract).then_inc(s_alo, 1)

            def sample_lo():
                dve.wait_ge(s_ahi, 4)
                for f2 in range(2):
                    for half in range(2):
                        r = slice(64 * half, 64 * half + 64)
                        v = lambda t: t[r, 2 * f2:2 * f2 + 2, SEQ:TOK].rearrange("p f (b i) -> p f b i", b=NB)
                        dve.tensor_tensor(v(HAL), sample_out(f2, half), v(HAH).bitcast(F32), ALU.subtract).then_inc(s_alo, 1)
            queries(0)
            for s in range(ITEMS + 2):
                if s + 1 < NB:
                    queries(s + 1)
                if s < ITEMS:
                    maximum(s)
                if 1 <= s <= NB:
                    normalise(s - 1)
                if s == NB + 1:
                    sample_lo()
                if s >= NB + AH + 1 and (s - 1) % AH == 0:
                    rows((s - 1 - NB) // AH - 1)
                if s >= NB + AH + 2 and (s - 2) % AH == 0:
                    back((s - 2 - NB) // AH - 1)
            back(PT_TILES - 1)

        def ln_pe(pe, T):
            pe.wait_ge(s_alo, 4 + PT_TILES)
            for n in range(N3):
                for j in range(AB):
                    mm = nc.tensor.matmul(PS[:, n, 0:TH], ones[:, :], Y[:, j, third(n)], start=(j == 0), stop=(j == AB - 1))
                mm.then_inc(s_ms, 1)
            for n in range(N3):
                T.add("sq", 1)
                pe.wait_ge(s_sq, T("sq"))
                for tt in range(TPT):
                    for j in range(AB):
                        mm = nc.tensor.matmul(PS[:, 7, 3 * n + tt:3 * n + tt + 1], SQ[:, j, tile(tt)], ones[:, 0:1],
                                              start=(j == 0), stop=(j == AB - 1))
                mm.then_inc(s_ms, 1)
                T.add("dg")
                pe.wait_ge(s_dg, T("dg"))
                nc.tensor.matmul(PS[:, 4 + n, 0:TH], ones[:, :], HF[:, 0, :], start=True, stop=True).then_inc(s_rb, 1)

        def ln_dve(dve, T):
            dve.wait_ge(s_ms, T_MS + N3)
            for n in range(N3):
                for j in range(AB):
                    y = Y[:, j, third(n)]
                    ins = dve.scalar_tensor_tensor(out=y, in0=PS[:, n, 0:TH], scalar=-1.0 / AW, in1=y, op0=ALU.mult, op1=ALU.add)
                ins.then_inc(s_yc, 1)
            for n in range(N3):
                T.add("rt")
                dve.wait_ge(s_rt, T("rt"))
                if n:
                    dve.wait_ge(s_rb, T("rb_made"))
                T.add("rb_made")
                link(dve, T, dve.reciprocal(ri[:, 3 * n:3 * n + 3], rt[:, 3 * n:3 * n + 3]))
                dve.tensor_tensor(HF[:, 0, :].rearrange("p (a b) -> p a b", b=P), ident[:, :].unsqueeze(1).to_broadcast([P, TPT, P]),
                                  ri[:, 3 * n:3 * n + 3].unsqueeze(2).to_broadcast([P, TPT, P]), ALU.mult).then_inc(s_dg, 1)
                T.add("rb")
                dve.wait_ge(s_rb, T("rb"))
                y = Y[:, :, third(n)]
                dve.tensor_tensor(y, y, PS[:, 4 + n, 0:TH].unsqueeze(1).to_broadcast([P, AB, TH]), ALU.mult).then_inc(s_yc, 1)
            for n in range(N3):
                T.add("hhi")
                dve.wait_ge(s_hhi, T("hhi"))
                dve.tensor_tensor(HBL[:, :, third(n)], Y[:, :, third(n)], HBH[:, :, third(n)].bitcast(F32),
                                  ALU.subtract).then_inc(s_hlo, 1)
                T.add("hlo")

        def ln_act(act, T):
            act.wait_ge(s_o, ITEMS)
            act.wait_ge(s_out, 32)
            act.wait_ge(s_att, PT_TILES)
            T.add("ms", N3)
            for n in range(N3):
                act.wait_ge(s_yc, n + 1)
                need(act, s_ms, T("ms"))
                act.activation(SQ[:, 0:AB, :], Y[:, :, third(n)], ACT.Square).then_inc(s_sq, 1)
                T.add("ms")
                act.wait_ge(s_ms, T("ms"))
                act.activation(rt[:, 3 * n:3 * n + 3], PS[:, 7, 3 * n:3 * n + 3], ACT.Sqrt,
                               bias=eps[:, 0:1], scale=1.0 / AW).then_inc(s_rt, 1)
            for n in range(N3):
                act.wait_ge(s_yc, N3 + n + 1)
                for j in range(AB):
                    y = Y[:, j, third(n)]
                    ins = act.activation(y, y, ACT.Silu, bias=sm("lb", j), scale=sm("lg", j))
                ins.then_inc(s_hf, 1)
                T.add("hf")
                act.wait_ge(s_hf, T("hf"))
                act.activation(HBH[:, :, third(n)], Y[:, :, third(n)], ACT.Copy).then_inc(s_hhi, 1)

        C_ORDER = [(k, n) for k in "fqvg" for n in range(N3)]
        C_SLOT = dict(f=0, q=1, v=2, g=1)
        C_LAST = {(k, n): C_ORDER[i - 2] for i, (k, n) in enumerate(C_ORDER)}

        def level_tiles(lv, n):
            hi = NT if lv <= SLEVELS else PT_TILES
            return range(TPT * n, min(TPT * n + TPT, hi))

        def state_bank(b):
            return PS[:, 6 + b // 2 % 2, tile(2 * (b // 4) + b % 2)]

        def c_pe(pe, T):
            def proj(k, n, p, ready):
                if n == 0:
                    have(pe, T, C_SLOT[k])
                if ready and k == "f":
                    ready(n)
                lk, ln = C_LAST[(k, n)]
                done = T("head") * N3 + ln + 1 - (N3 if (lk, k) == ("g", "f") else 0)
                need(pe, s_cg[lk], done)
                product(PS[:, (C_ORDER.index((k, n))) % 2, 0:TH], C_SLOT[k], n).then_inc(s_cf[k], 1)

            def vturn(n, p):
                need(pe, s_cg["v"], T("head") * N3 + n + 1)
                need(pe, s_vk, T("vk"))
                T.add("vk")
                if n == 0:
                    need(pe, s_cr, T("hgrn"))
                for tt in range(TPT):
                    mm = nc.tensor.transpose(PS[:, 2, tile(tt)], VT[:, n, tile(tt)], ident[:, :])
                mm.then_inc(s_vt, 1)

            def level(lv, p):
                T.add("up")
                need(pe, s_up, T("up"))
                for n in range(N3):
                    if lv == 0:
                        need(pe, s_cn, T("hgrn") * N3)
                    else:
                        need(pe, s_mg, T("mg") - 2)
                    T.add("mg")
                    for t in level_tiles(lv, n):
                        mm = nc.tensor.matmul(PS[:, 3 + n, tile(t % TPT)], KC[:, tile(t)], QC[:, p, tile(t)],
                                              start=True, stop=True)
                    mm.then_inc(s_lv, 1)

            def kturn(n):
                T.add("kt")
                need(pe, s_up, T("up") + 1)
                need(pe, s_mg, T("mg") - 2 + n)
                for tt in range(TPT):
                    mm = nc.tensor.transpose(PS[:, 3 + n, tile(tt)], KC[:, tile(TPT * n + tt)], ident[:, :])
                mm.then_inc(s_kt, 1)

            def states(p):
                need(pe, s_kd, T("kt"))
                need(pe, s_sn, T("hgrn") * NB)
                for c in range(PT_TILES):
                    mm = nc.tensor.matmul(PS[:, 6 + c // 4, tile(c % 4)], KD[:, c, :], VC[:, p, c, :], start=True, stop=True)
                mm.then_inc(s_st, 1)

            def sample_states():
                need(pe, s_ss, T("hgrn") * PT_TILES + PT_TILES)
                need(pe, s_vm, T("hgrn") + 1)
                for b in range(NB):
                    if b == NB // 2:
                        T.add("sf")
                        mm.then_inc(s_sf, 1)
                        need(pe, s_sf, T("sf"))
                    r = slice(32 * (b // 2), 32 * (b // 2) + 32)
                    mm = nc.tensor.matmul(state_bank(b), KD[r, NT - 1, :], VM[r, b % 2, :], start=True, stop=True)
                mm.then_inc(s_sm, 1)

            def outputs(n, p):
                if n == 0:
                    need(pe, s_mg, T("mg"))
                    need(pe, s_ss, (T("hgrn") + 1) * PT_TILES)
                    need(pe, s_s0, (T("hgrn") + 1) * 16)
                for t in range(TPT * n, TPT * n + TPT):
                    out = PS[:, 3 + n, tile(t % TPT)]
                    mm = nc.tensor.matmul(out, VC[:, p, t, :], AM[:, t, :], start=True, stop=(t in (0, PT_TILES)))
                    if 0 < t < PT_TILES:
                        mm = nc.tensor.matmul(out, SS[:, t - 1, :], QC[:, p, tile(t)], start=False, stop=True)
                    if t == PT_TILES:
                        for b in range(NB):
                            mm = nc.tensor.matmul(out[:, NS * b:NS * (b + 1)], S0[:, b, :],
                                                  QC[:, p, SEQ + NS * b:SEQ + NS * (b + 1)], start=False, stop=True,
                                                  skip_group_check=True)
                mm.then_inc(s_oc, 1)

            def norm_sums():
                need(pe, s_oq, T("hgrn") * N3 + N3)
                need(pe, s_vk, T("vk"))
                for t in range(NT):
                    mm = nc.tensor.matmul(PS[:, 2, TH + t:TH + t + 1], AM[:, t, :], ones[:, 0:1], start=True, stop=True)
                mm.then_inc(s_cm, 1)

            def norm_cast():
                need(pe, s_cd, T("hgrn") + 1)
                need(pe, s_og, T("hgrn") * N3 + N3)
                for n in range(N3):
                    mm = nc.tensor.matmul(PS[:, 3 + n, 0:TH], ones[:, :],
                                          KD[:, TPT * n:TPT * n + TPT, :].rearrange("p a b -> p (a b)"), start=True, stop=True)
                    mm.then_inc(s_cb, 1)

            def step(pp, hp, ready=None):
                for i, (k, n) in enumerate(C_ORDER):
                    if pp is not None:
                        proj(k, n, pp, ready)
                        if k == "v" and n:
                            vturn(n - 1, pp)
                        if k == "g" and n == 0:
                            vturn(N3 - 1, pp)
                    if hp is None:
                        continue
                    if i <= LEVELS:
                        level(i, hp)
                    if i == 8:
                        for m in range(N3):
                            kturn(m)
                        states(hp)
                    if i == 9:
                        for m in range(N3):
                            outputs(m, hp)
                        sample_states()
                    if i == 10:
                        norm_sums()
                    if i == 11:
                        norm_cast()
                if pp is not None:
                    T.add("head")
                if hp is not None:
                    T.add("up")
                    T.add("hgrn")
            step(0, None, lambda n: pe.wait_ge(s_hlo, H_F0 + 2 * (n + 1)))
            step(1, 0)
            with pe.Fori(0, CH // 2 - 1) as i:
                T.enter(i, w0=2, w1=4, w2=2, up=2 * (LEVELS + 2), mg=2 * N3 * (LEVELS + 1), kt=2 * N3, vk=2 * N3, head=2, hgrn=2, sf=2)
                step(0, 1)
                step(1, 0)
                T.leave(CH // 2 - 1)
            step(None, 1)

        def c_act(act, T):
            def take(k, n, p, h):
                count = T("head") * N3 + n + 1
                if n == 0:
                    slot, last = {"f": (1, "g"), "q": (2, "v"), "v": (1, "q"), "g": (0, "f")}[k]
                    prev = T("head") * N3 + (0 if k in "fq" else N3)
                    cut_hi(act, T, slot, (s_cf[last], prev))
                need(act, s_cf[k], count)
                src = PS[:, C_ORDER.index((k, n)) % 2, 0:TH]
                if k == "f":
                    if n == 0:
                        need(act, s_mg, (T("head") - 1) * N3 * (LEVELS + 1))
                    act.activation(FG[:, p, third(n)], src, ACT.Sigmoid).then_inc(s_cg[k], 1)
                elif k == "q":
                    if n == 0:
                        need(act, s_oc, (T("head") - 1) * N3)
                    act.activation(QC[:, p, third(n)], src, ACT.Copy).then_inc(s_cg[k], 1)
                elif k == "v":
                    need(act, s_vt, count - N3)
                    act.activation(VT[:, n, :], src, ACT.Copy).then_inc(s_cg[k], 1)
                else:
                    act.activation(X[:, h, third(n)], src, ACT.Sigmoid).then_inc(s_gs, 1)

            def vtake(n, p):
                need(act, s_vt, T("head") * N3 + n + 1)
                if n == 0:
                    need(act, s_vm, T("head") - 1)
                act.activation(VC[:, p, TPT * n:TPT * n + TPT, :], PS[:, 2, 0:TH].rearrange("p (a b) -> p a b", b=P),
                               ACT.Copy).then_inc(s_vk, 1)

            def ktake(n):
                need(act, s_kt, T("hgrn") * N3 + n + 1)
                act.activation(KD[:, TPT * n:TPT * n + TPT, :], PS[:, 3 + n, 0:TH].rearrange("p (a b) -> p a b", b=P),
                               ACT.Copy).then_inc(s_kd, 1)

            def square(n):
                need(act, s_oc, T("hgrn") * N3 + n + 1)
                act.activation(AM[:, TPT * n:TPT * n + TPT, :], PS[:, 3 + n, 0:TH].rearrange("p (a b) -> p a b", b=P),
                               ACT.Square).then_inc(s_oq, 1)

            def root():
                need(act, s_cm, T("hgrn") + 1)
                act.activation(rt[:, 0:NT], PS[:, 2, TH:TH + NT], ACT.Sqrt, bias=eps[:, 0:1], scale=1.0 / P).then_inc(s_cr, 1)

            def load_state(h):
                need(act, s_hgs, T("hgrn") * 16)
                act.dma_start(S0[:, :, :], state_d[h]).then_inc(s_s0, 16)

            def store_states(h):
                need(act, s_ss, (T("hgrn") + 1) * PT_TILES)
                act.dma_start(hgp_o[h], SS[:, PT_TILES - 1, :]).then_inc(s_hgp, 16)
                need(act, s_sn, (T("hgrn") + 1) * NB)
                act.dma_start(hgs_o[h], S0[:, :, :]).then_inc(s_hgs, 16)

            def step(pp, hp, h):
                for i, (k, n) in enumerate(C_ORDER):
                    if hp is not None and i == 2:
                        load_state(h - 1)
                    if pp is not None:
                        take(k, n, pp, h)
                        if k == "v" and n:
                            vtake(n - 1, pp)
                        if k == "g" and n == 0:
                            vtake(N3 - 1, pp)
                    if hp is None:
                        continue
                    if i == 8:
                        for m in range(N3):
                            ktake(m)
                    if i == 9:
                        for m in range(N3):
                            square(m)
                    if i == 11:
                        root()
                        store_states(h - 1)
                if pp is not None:
                    T.add("head")
                if hp is not None:
                    T.add("hgrn")
            act.wait_ge(s_sp, 16)
            step(0, None, 0)
            step(1, 0, 1)
            with act.Fori(0, CH // 2 - 1) as i:
                T.enter(i, w0=2, w1=4, w2=2, head=2, hgrn=2)
                step(0, 1, 2 * i + 2)
                step(1, 0, 2 * i + 3)
                T.leave(CH // 2 - 1)
            step(None, 1, CH)

        def c_dve(dve, T):
            def gate(n, h):
                T.add("gs")
                need(dve, s_gs, T("gs"))
                o = X[:, h, third(n)]
                dve.tensor_tensor(o, o, PS[:, C_ORDER.index(("g", n)) % 2, 0:TH], ALU.mult).then_inc(s_cg["g"], 1)

            def start(p, h):
                need(dve, s_cg["f"], (T("hgrn") + 1) * N3)
                need(dve, s_cg["q"], (T("hgrn") + 1) * N3)
                need(dve, s_kt, T("hgrn") * N3)
                link(dve, T, dve.tensor_scalar(FG[:, p, :], FG[:, p, :], low[:, 5, bass.ds(h, 1)], low[:, 4, bass.ds(h, 1)],
                                               ALU.mult, ALU.add))
                dve.tensor_scalar(KC[:, :], FG[:, p, :], -1.0, 1.0, ALU.mult, ALU.add).then_inc(s_up, 1)

            def totals(lv):
                return TA if lv % 2 else TB

            def level(lv, p):
                T.add("lv", N3)
                need(dve, s_lv, T("lv"))
                if lv == 0:
                    q = QC[:, p, :]
                    dve.tensor_tensor(q, q, FG[:, p, :], ALU.mult).then_inc(s_up, 1)
                else:
                    cols = TOK if lv <= SLEVELS else SEQ
                    w = 1 << (lv - 1)
                    nb = cols // (2 * w)
                    two = lambda ap: ap.rearrange("p (b two w) -> p b two w", two=2, w=w)
                    src = (FG[:, p, 0:cols] if lv == 1 else totals(lv - 1)[:, 0:cols // w])
                    pair = src.rearrange("p (b two) -> p b two", two=2)
                    qv, kv = two(QC[:, p, 0:cols]), two(KC[:, 0:cols])
                    dve.tensor_tensor(qv[:, :, 1, :], qv[:, :, 1, :], pair[:, :, 0].unsqueeze(2).to_broadcast([P, nb, w]), ALU.mult)
                    dve.tensor_tensor(kv[:, :, 0, :], kv[:, :, 0, :], pair[:, :, 1].unsqueeze(2).to_broadcast([P, nb, w]),
                                      ALU.mult).then_inc(s_up, 1)
                for n in range(N3):
                    tiles = level_tiles(lv, n)
                    nt = len(tiles)
                    a = AM[:, tiles.start:tiles.stop, :]
                    ps = PS[:, 3 + n, 0:nt * P].rearrange("p (a b) -> p a b", b=P)
                    if lv == 0:
                        ins = dve.tensor_tensor(a, ps, ident[:, :].unsqueeze(1).to_broadcast([P, nt, P]), ALU.mult)
                    else:
                        ins = dve.copy_predicated(a, lvl_mask[:, lv - 1, :].unsqueeze(1).to_broadcast([P, nt, P]), ps)
                    ins.then_inc(s_mg, 1)
                    T.add("mg")
                if lv:
                    out = TS[:, NB:2 * NB] if lv == LEVELS else totals(lv)[:, 0:nb]
                    ins = dve.tensor_tensor(out, pair[:, :, 0], pair[:, :, 1], ALU.mult)
                    if lv == SLEVELS:
                        link(dve, T, ins)
                        ins = dve.tensor_copy(TS[:, 0:NB], out[:, SEQ // NS:TOK // NS])
                    link(dve, T, ins)

            def mask_values(p):
                need(dve, s_vk, (T("hgrn") + 1) * N3)
                for e in range(2):
                    ins = dve.tensor_scalar(VM[:, e, :], VC[:, p, NT - 1, :], parity[:, e:e + 1], None, ALU.mult)
                ins.then_inc(s_vm, 1)

            def states():
                need(dve, s_st, T("hgrn") + 1)
                need(dve, s_hgp, T("hgrn") * 16)
                for c in range(PT_TILES):
                    ps = PS[:, 6 + c // 4, tile(c % 4)]
                    if c == 0:
                        ins = dve.tensor_copy(SS[:, 0, :], ps)
                    else:
                        need(dve, s_ss, T("ss"))
                        ins = dve.scalar_tensor_tensor(out=SS[:, c, :], in0=SS[:, c - 1, :], scalar=TS[:, NB + c:NB + c + 1],
                                                       in1=ps, op0=ALU.mult, op1=ALU.add)
                    ins.then_inc(s_ss, 1)
                    T.add("ss")

            def gated(n, h):
                need(dve, s_oc, T("hgrn") * N3 + n + 1)
                need(dve, s_oq, T("hgrn") * N3 + n + 1)
                o = X[:, h, third(n)]
                dve.tensor_tensor(o, o, PS[:, 3 + n, 0:TH], ALU.mult).then_inc(s_og, 1)

            def sample_states():
                need(dve, s_sm, T("hgrn") + 1)
                for b in range(NB):
                    dve.scalar_tensor_tensor(out=S0[:, b, :], in0=S0[:, b, :], scalar=TS[:, b:b + 1],
                                             in1=state_bank(b), op0=ALU.mult, op1=ALU.add).then_inc(s_sn, 1)

            def diagonal():
                need(dve, s_cr, T("hgrn") + 1)
                link(dve, T, dve.reciprocal(ri[:, 0:NT], rt[:, 0:NT]))
                dve.tensor_tensor(KD[:, :, :], ident[:, :].unsqueeze(1).to_broadcast([P, NT, P]),
                                  ri[:, 0:NT].unsqueeze(2).to_broadcast([P, NT, P]), ALU.mult).then_inc(s_cd, 1)

            def finish(h):
                for n in range(N3):
                    need(dve, s_cb, T("hgrn") * N3 + n + 1)
                    o = X[:, h, third(n)]
                    dve.scalar_tensor_tensor(out=o, in0=o, scalar=sm("gn"), in1=PS[:, 3 + n, 0:TH], op0=ALU.mult,
                                             op1=ALU.mult).then_inc(s_cn, 1)

            def step(pp, hp, h):
                if hp is not None:
                    start(hp, h - 1)
                for i, (k, n) in enumerate(C_ORDER):
                    if pp is not None and n == 0:
                        cut_lo(dve, T, {"f": 1, "q": 2, "v": 1, "g": 0}[k])
                    if hp is not None:
                        if i <= LEVELS:
                            level(i, hp)
                        if i == 8:
                            mask_values(hp)
                            states()
                        if i == 9:
                            for m in range(N3):
                                gated(m, h - 1)
                            sample_states()
                        if i == 11:
                            diagonal()
                    if pp is not None and k == "g":
                        gate(n, h)
                if hp is not None:
                    finish(h - 1)
                    T.add("hgrn")
            step(0, None, 0)
            step(1, 0, 1)
            with dve.Fori(0, CH // 2 - 1) as i:
                T.enter(i, hi=8, gs=2 * N3, dc=2 * (1 + LEVELS + 1 + 1), lv=2 * N3 * (LEVELS + 1), mg=2 * N3 * (LEVELS + 1),
                        ss=2 * PT_TILES, hgrn=2)
                step(0, 1, 2 * i + 2)
                step(1, 0, 2 * i + 3)
                T.leave(CH // 2 - 1)
            step(None, 1, CH)

        def cut_o_act(act, T):
            act.wait_ge(s_cf["g"], N3 * CH)
            act.wait_ge(s_cn, N3 * CH)
            for n in range(N3):
                for half, hi in ((0, HAH), (1, HBH)):
                    act.activation(hi[:, :, third(n)], X[:, half * AB:(half + 1) * AB, third(n)], ACT.Copy).then_inc(s_hhi, 1)

        def cut_o_dve(dve, T):
            for n in range(N3):
                for half, hi, lo in ((0, HAH, HAL), (1, HBH, HBL)):
                    T.add("hhi")
                    dve.wait_ge(s_hhi, T("hhi"))
                    dve.tensor_tensor(lo[:, :, third(n)], X[:, half * AB:(half + 1) * AB, third(n)],
                                      hi[:, :, third(n)].bitcast(F32), ALU.subtract).then_inc(s_hlo, 1)
                    T.add("hlo")

        s_gs = sem("s_gs")
        s_low = sem("s_low")
        s_lowe = sem("s_lowe")
        T_MS = N3

        block = ctx.enter_context(nc.Block())

        @block.sync
        def _(sp):
            sync_program(sp)

        @block.gpsimd
        def _(pool):
            pool_program(pool)

        @block.tensor
        def _(pe):
            T = Tally()
            pe.wait_ge(s_const, 3)
            norm_pe(pe, T)
            ab_pe(pe, T)
            att_pe(pe, T)
            ln_pe(pe, T)
            proj_pe(pe, T, lambda n: pe.wait_ge(s_hlo, H_AB + n + 1))
            norm_pe(pe, T)
            ffn_pe(pe, T, lambda n: pe.wait_ge(s_hlo, H_ABO + 2 * (n + 1)))
            norm_pe(pe, T)
            c_pe(pe, T)
            proj_pe(pe, T, lambda n: pe.wait_ge(s_hlo, H_C + 2 * (n + 1)))
            norm_pe(pe, T)
            ffn_pe(pe, T, lambda n: pe.wait_ge(s_hlo, H_CO + 2 * (n + 1)))
            norm_pe(pe, T)

        @block.scalar
        def _(act):
            T = Tally()
            act.wait_ge(s_small, 16)
            act.wait_ge(s_low, 1)
            norm_act(act, T, 0)
            cut_hi(act, T, 0)
            ab_act(act, T)
            att_act(act, T)
            ln_act(act, T)
            proj_act(act, T)
            norm_act(act, T, X_AB)
            ffn_act(act, T)
            cut_hi(act, T, 0, (s_xo, T("x")))
            norm_act(act, T, XC_START)
            act.wait_ge(s_low, 3)
            act.activation(low[:, 0:2, :], low[:, 0:2, :], ACT.Exp).then_inc(s_lowe, 1)
            c_act(act, T)
            cut_o_act(act, T)
            proj_act(act, T)
            norm_act(act, T, X_C)
            ffn_act(act, T)
            norm_act(act, T, X_END, final=True)

        @block.vector
        def _(dve):
            T = Tally()
            dve.memset(eps[:, :], EPS).then_inc(s_low, 1)
            dve.wait_ge(s_small, 16)
            dve.wait_ge(s_const, 4)
            link(dve, T, dve.tensor_scalar(parity_i[:, 1:2], parity_i[:, 0:1], 4, 1, ALU.logical_shift_right, ALU.bitwise_and))
            link(dve, T, dve.tensor_copy(parity[:, 1:2], parity_i[:, 1:2]))
            link(dve, T, dve.tensor_scalar(parity[:, 0:1], parity[:, 1:2], -1.0, 1.0, ALU.mult, ALU.add))
            l0, l1 = sm("low", 0, CH), sm("low", CH, CH)
            link(dve, T, dve.tensor_tensor(low[:, 2, :], l0, l1, ALU.max))
            dve.tensor_tensor(low[:, 0, :], l0, low[:, 2, :], ALU.subtract).then_inc(s_low, 1)
            dve.tensor_tensor(low[:, 1, :], l1, low[:, 2, :], ALU.subtract).then_inc(s_low, 1)
            norm_dve(dve, T, 0)
            cut_lo(dve, T, 0)
            ab_dve(dve, T)
            att_dve(dve, T)
            ln_dve(dve, T)
            proj_dve(dve, T, 1)
            norm_dve(dve, T, 2)
            ffn_dve(dve, T)
            cut_lo(dve, T, 0)
            norm_dve(dve, T, 1)
            dve.wait_ge(s_lowe, 1)
            link(dve, T, dve.tensor_tensor(low[:, 3, :], low[:, 0, :], low[:, 1, :], ALU.add))
            link(dve, T, dve.reciprocal(low[:, 2, :], low[:, 3, :]))
            link(dve, T, dve.tensor_tensor(low[:, 4, :], low[:, 1, :], low[:, 2, :], ALU.mult))
            link(dve, T, dve.tensor_scalar(low[:, 5, :], low[:, 4, :], -1.0, 1.0, ALU.mult, ALU.add))
            c_dve(dve, T)
            cut_o_dve(dve, T)
            proj_dve(dve, T, 2)
            norm_dve(dve, T, 3)
            ffn_dve(dve, T)
            norm_dve(dve, T, 4, final=True)


def kernel(x_prompt, x_sample, cache_a_k, cache_a_v, state_conv, state_hgrn, attn_norm, ffn_norm, final_norm,
           w_in_ab, rel_bias, conv_w, conv_b, conv_ln_g, conv_ln_b, w_out_ab, w_in_c, lower_bounds, c_norm_g,
           w_out_c, ffn_w_in, ffn_w_out):
    import numpy as np
    import concourse.bacc as bacc
    from concourse.bass_utils import run_bass_kernel_spmd

    a = np.asarray
    x = np.concatenate([a(x_prompt).reshape(SEQ, D), a(x_sample).reshape(NB * NS, D)])
    by_block = lambda v: a(v).reshape(-1, P).T
    tiles = lambda w: a(w).reshape(KT, P, -1, P).transpose(2, 1, 0, 3).reshape(-1, P, D)
    fi = a(ffn_w_in).reshape(2, KT, P, 2, FJ, P).transpose(0, 4, 3, 2, 1, 5)
    small = np.concatenate([
        a(conv_w)[0].T.reshape(AB, P, CW).transpose(1, 0, 2).reshape(P, AB * CW),
        by_block(conv_b[0]), by_block(conv_ln_g[0]), by_block(conv_ln_b[0]),
        by_block(attn_norm[0]), by_block(attn_norm[1]), by_block(ffn_norm[0]), by_block(ffn_norm[1]),
        by_block(final_norm), by_block(lower_bounds[0]), by_block(lower_bounds[1]), by_block(c_norm_g[0])], axis=1)
    ins = {
        "x_t": x.T.reshape(KT, P, TOK).transpose(1, 0, 2).reshape(P, KT * TOK),
        "w_ab": tiles(w_in_ab[0]), "w_oab": tiles(w_out_ab[0]), "w_c": tiles(w_in_c[0]), "w_oc": tiles(w_out_c[0]),
        "w_fi": fi.reshape(4 * FJ, P, D), "w_fo": a(ffn_w_out).reshape(2 * FJ, P, D),
        "small": small, "rel": a(rel_bias)[0][:, ::-1],
        "k_cache": a(cache_a_k)[0].transpose(0, 2, 3, 1).reshape(NB, AB, P, CACHE).transpose(0, 2, 1, 3),
        "v_cache": a(cache_a_v)[0].reshape(NB, 4, P, AW).transpose(0, 2, 1, 3),
        "hist": a(state_conv)[0].transpose(2, 0, 1).reshape(AB, P, NB, HIST).transpose(1, 0, 2, 3),
        "state": a(state_hgrn)[0].transpose(1, 2, 0, 3),
    }
    outs = {
        "y": (P, KT * TOK), "k_new": (P, AB, CACHE + P), "v_new": (P, 5, AW), "conv_p": (P, AB, HIST),
        "conv_s": (P, AB, NB, HIST), "hg_p": (CH, P, P), "hg_s": (CH, P, NB, P),
    }
    nc = bacc.Bacc("TRN2", target_bir_lowering=False, num_devices=1)
    ins = {k: np.ascontiguousarray(v) for k, v in ins.items()}
    args = [nc.dram_tensor(k + "_in", v.shape, F32, kind="ExternalInput").ap() for k, v in ins.items()]
    args += [nc.dram_tensor(k + "_out", s, F32, kind="ExternalOutput").ap() for k, s in outs.items()]
    encoder(nc, *args)
    r = run_bass_kernel_spmd(nc, [{k + "_in": v for k, v in ins.items()}], core_ids=[0]).results[0]
    y, kn, vn, cp, cs, hp, hs = (r[k + "_out"] for k in outs)
    y = y.reshape(P, KT, TOK).transpose(2, 1, 0).reshape(TOK, D)
    kn = kn.transpose(2, 1, 0).reshape(CACHE + P, AH, AD)
    vn = vn.transpose(1, 0, 2).reshape(CACHE + P, AH, AD)
    return (y[:SEQ].reshape(1, SEQ, D), y[SEQ:].reshape(NB, NS, D),
            kn[:CACHE].reshape(1, 1, CACHE, AH, AD), vn[:CACHE].reshape(1, 1, CACHE, AH, AD),
            cp.transpose(2, 1, 0).reshape(1, 1, HIST, AW), hp.reshape(1, 1, CH, P, P),
            kn[CACHE:].reshape(1, NB, NS, AH, AD), vn[CACHE:].reshape(1, NB, NS, AH, AD),
            cs.transpose(2, 3, 1, 0).reshape(1, NB, HIST, AW),
            hs.transpose(2, 0, 1, 3).reshape(1, NB, CH, P, P))
```

```python
import numpy as np
from contextlib import ExitStack

import concourse.bass as bass
from concourse import mybir

F32 = mybir.dt.float32
F32R = mybir.dt.float32r
I32 = mybir.dt.int32
U8 = mybir.dt.uint8
ALU = mybir.AluOpType
ACT = mybir.ActivationFunctionType
AX = mybir.AxisListType

P = 128
D = 1024
KT = D // P
SEQ = 1024
NB = 8
NS = 16
TOK = SEQ + NB * NS
NT = TOK // P
PT_TILES = SEQ // P
TH = 384
N3 = TOK // TH
TPT = TH // P
AH, AD = 8, 64
AW = AH * AD
AB = AW // P
CACHE = 512
CW = 31
HIST = CW - 1
CH = 8
FF = 2816
FJ = FF // P
NCH = FJ // 2
EPS = 1e-6
NEG = -1e30
LEVELS = 7
SLEVELS = 4
SMALL = dict(cw=(0, AB * CW), cb=(124, AB), lg=(128, AB), lb=(132, AB), gain=(136, 5 * KT),
             low=(176, 2 * CH), gn=(192, 1))
NSMALL = 193


class Tally:

    def __init__(self):
        self.base, self.now, self.step, self.i = {}, {}, {}, None

    def __call__(self, name):
        n = self.base.get(name, 0) + self.now.get(name, 0)
        if self.i is not None and self.step.get(name, 0):
            return self.i * self.step[name] + n
        return n

    def add(self, name, k=1):
        self.now[name] = self.now.get(name, 0) + k

    def enter(self, i, **step):
        for k, v in self.now.items():
            self.base[k] = self.base.get(k, 0) + v
        self.now, self.step, self.i = {}, step, i

    def leave(self, times):
        assert {k: v for k, v in self.now.items() if v} == {k: v for k, v in self.step.items() if v}, (self.now, self.step)
        for k, v in self.step.items():
            self.base[k] = self.base.get(k, 0) + v * times
        self.now, self.step, self.i = {}, {}, None


def need(eng, sem, value):
    if isinstance(value, int) and value <= 0:
        return
    eng.wait_ge(sem, value)


def encoder(nc, x_t, w_ab, w_oab, w_c, w_oc, w_fi, w_fo, small_d, rel_d, kc_d, vc_d, hist_d, state_d,
            y_o, k_o, v_o, cvp_o, cvs_o, hgp_o, hgs_o):
    with ExitStack() as ctx:
        sb = lambda name, shape, dt=F32: ctx.enter_context(nc.sbuf_tensor(name, shape, dt))
        sem = lambda name: ctx.enter_context(nc.semaphore(name))

        X = sb("X", [P, KT, TOK])
        HAH = sb("HAH", [P, AB, TOK], F32R)
        HAL = sb("HAL", [P, AB, TOK], F32R)
        with nc.sbuf_tensor("CACHES", [P, KT * TOK], F32) as CACHES:
            pass
        HBH = sb("HBH", [P, AB, TOK], F32R)
        HBL = sb("HBL", [P, AB, TOK], F32R)
        WR = sb("WR", [P, 3, D])
        WH = sb("WH", [P, 3, D], F32R)
        WL = sb("WL", [P, 3, D], F32R)
        small = sb("small", [P, NSMALL])
        ident = sb("ident", [P, P])
        ones = sb("ones", [P, P])
        lvl_mask = sb("lvl_mask", [P, LEVELS, P], U8)
        low = sb("low", [P, 6, CH])
        parity_i = sb("parity_i", [P, 3], I32)
        parity = sb("parity", [P, 2])
        rt = sb("rt", [P, 16])
        ri = sb("ri", [P, 16])
        nmax = sb("nmax", [P, 2])
        psum_ = sb("psum_", [P, 4])
        rsum = sb("rsum", [P, 2])
        late = sb("late", [1, P])
        plus = sb("plus", [1, 64])
        eps = sb("eps", [P, 1])
        with ExitStack() as c2:
            s2 = lambda name, shape, dt=F32: c2.enter_context(nc.sbuf_tensor(name, shape, dt))
            HF1 = s2("HF1", [P, KT, TH])
            s2("norm_gap", [P, 6 * TOK - KT * TH])
            HF0 = s2("HF0", [P, KT, TH])
            SQ = s2("SQ", [P, KT, TH])
            DG = s2("DG", [P, TPT, P])
        with ExitStack() as c2:
            s2 = lambda name, shape, dt=F32: c2.enter_context(nc.sbuf_tensor(name, shape, dt))
            VTOK = s2("VTOK", [P, NT, AW])
            Y = s2("Y", [P, AB, TOK])
            with ExitStack() as c3:
                s3 = lambda name, shape, dt=F32: c3.enter_context(nc.sbuf_tensor(name, shape, dt))
                EV = s3("EV", [P, N3, TH])
                UP = s3("UP", [P, HIST + SEQ])
                US = s3("US", [P, AB, NB, HIST + NS])
                CO = s3("CO", [P, AB, HIST])
            BT = s2("BT", [P, AH, 2 * P])
            with ExitStack() as c3:
                s3 = lambda name, shape, dt=F32: c3.enter_context(nc.sbuf_tensor(name, shape, dt))
                LSQ = s3("LSQ", [P, AB, TH])
                LDG = s3("LDG", [P, TPT, P])
            PR = s2("PR", [P, 2, 5 * P])
            PRT = s2("PRT", [P, 2, 5 * P])
            OS = s2("OS", [P, AW])
            BS = s2("BS", [P, P + NS])
        with ExitStack() as c2:
            s2 = lambda name, shape, dt=F32: c2.enter_context(nc.sbuf_tensor(name, shape, dt))
            UH = s2("UH", [P, 2, 2, TOK], F32R)
            UL = s2("UL", [P, 2, 2, TOK], F32R)
            SG = s2("SG", [P, N3, TH])
            UF = s2("UF", [P, N3, TH])
        with ExitStack() as c2:
            s2 = lambda name, shape, dt=F32: c2.enter_context(nc.sbuf_tensor(name, shape, dt))
            FG = s2("FG", [P, 2, TOK])
            QC = s2("QC", [P, 2, TOK])
            VC = s2("VC", [P, 2, NT, P])
            KC = s2("KC", [P, TOK])
            AM = s2("AM", [P, NT, P])
            TA = s2("TA", [P, TOK // 2])
            TB = s2("TB", [P, TOK // 4])
            TS = s2("TS", [P, 2 * NB])
            KD = s2("KD", [P, NT, P])
            VT = s2("VT", [P, N3, TH])
            S0 = s2("S0", [P, NB, P])
            SS = s2("SS", [P, PT_TILES, P])
            VM = s2("VM", [P, 2, P])
        PS = ctx.enter_context(nc.psum_tensor("PS", [P, 8, 512], F32))
        PSF = PS[:, :, :].rearrange("p b n -> p (b n)")
        xd = nc.dram_tensor("x_spill", [P, KT * TOK], F32).ap()
        padded = nc.dram_tensor("rel_padded", [AH, 512], F32)
        skewed = nc.dram_tensor("rel_skewed", [P, AH, 512], F32)

        KCA = CACHES[:, 0:4096].rearrange("p (s f n) -> p s f n", s=2, f=AB)
        VCA = CACHES[:, 4096:8192].rearrange("p (s f n) -> p s f n", s=2, f=AB)
        QB = CACHES[:, 8192:9216].rearrange("p (s f n) -> p s f n", s=2, f=AB)
        QT = lambda b: X[:, b, :]
        KTT = lambda b: X[:, AB + b, :]

        def sm(name, i=0, n=1):
            o = SMALL[name][0]
            return small[:, bass.ds(o + i, n)]

        def hh(k, cols):
            return HAH[:, k, cols] if k < AB else HBH[:, k - AB, cols]

        def hl(k, cols):
            return HAL[:, k, cols] if k < AB else HBL[:, k - AB, cols]

        third = lambda n: slice(n * TH, (n + 1) * TH)
        tile = lambda t: slice(t * P, (t + 1) * P)

        s_in = [sem(f"s_in{n}") for n in range(N3)]
        s_small = sem("s_small")
        s_hist = sem("s_hist")
        s_rel = sem("s_rel")
        s_pad = sem("s_pad")
        s_bt = sem("s_bt")
        s_bias = sem("s_bias")
        s_const = sem("s_const")
        s_dc = sem("s_dc")
        s_raw = [sem(f"s_raw{i}") for i in range(3)]
        s_hi = sem("s_hi")
        s_lo = [sem(f"s_lo{i}") for i in range(3)]
        s_sq = sem("s_sq")
        s_ms = sem("s_ms")
        s_fold = sem("s_fold")
        s_ps = sem("s_ps")
        s_rt = sem("s_rt")
        s_dg = sem("s_dg")
        s_rb = sem("s_rb")
        s_hf = sem("s_hf")
        s_hhi = sem("s_hhi")
        s_hlo = sem("s_hlo")
        s_full = {k: sem(f"s_full_{k}") for k in ("g", "a", "q", "k", "v", "vt")}
        s_got = {k: sem(f"s_got_{k}") for k in ("g", "a", "q", "k", "v", "vt")}
        s_cv = sem("s_cv")
        s_co = sem("s_co")
        s_kc = [sem(f"s_kc{i}") for i in range(2)]
        s_vc = [sem(f"s_vc{i}") for i in range(2)]
        s_qb = sem("s_qb")
        s_s = sem("s_s")
        s_nm = sem("s_nm")
        s_p = sem("s_p")
        s_rs = sem("s_rs")
        s_pn = sem("s_pn")
        s_pt = sem("s_pt")
        s_ptc = sem("s_ptc")
        s_o = sem("s_o")
        s_os = sem("s_os")
        s_ot = sem("s_ot")
        s_ahi = sem("s_ahi")
        s_alo = sem("s_alo")
        s_yc = sem("s_yc")
        s_x = sem("s_x")
        s_xo = sem("s_xo")
        s_xr = [sem(f"s_xr{i}") for i in range(2)]
        s_sp = sem("s_sp")
        s_fa = sem("s_fa")
        s_fb = sem("s_fb")
        s_si = sem("s_si")
        s_u = sem("s_u")
        s_uh = sem("s_uh")
        s_ul = sem("s_ul")
        s_cf = {k: sem(f"s_cf_{k}") for k in "fqvg"}
        s_cg = {k: sem(f"s_cg_{k}") for k in "fqvg"}
        s_vt = sem("s_vt")
        s_vk = sem("s_vk")
        s_lv = sem("s_lv")
        s_mg = sem("s_mg")
        s_up = sem("s_up")
        s_kt = sem("s_kt")
        s_kd = sem("s_kd")
        s_st = sem("s_st")
        s_ss = sem("s_ss")
        s_vm = sem("s_vm")
        s_s0 = sem("s_s0")
        s_sm = sem("s_sm")
        s_sf = sem("s_sf")
        s_sn = sem("s_sn")
        s_oc = sem("s_oc")
        s_oq = sem("s_oq")
        s_og = sem("s_og")
        s_cm = sem("s_cm")
        s_cr = sem("s_cr")
        s_cd = sem("s_cd")
        s_cb = sem("s_cb")
        s_cn = sem("s_cn")
        s_hgp = sem("s_hgp")
        s_hgs = sem("s_hgs")
        s_outc = sem("s_outc")
        s_out = sem("s_out")

        def weights(sp, T, slot, src):
            need(sp, s_lo[slot], T(f"w{slot}"))
            sp.dma_start(WR[:, slot, :], src).then_inc(s_raw[slot], 16)
            T.add(f"w{slot}")

        def ffn_sp(sp, T, layer):
            fi = lambda t: w_fi[t + layer * 2 * FJ, :, :]
            fo = lambda t: w_fo[t + layer * FJ, :, :]

            def w_in(c, slots=(0, 1, 2, 0)):
                for i, slot in enumerate(slots):
                    weights(sp, T, slot, fi(c * 4 + i))

            def w_out(c, slots=(1, 2)):
                for i, slot in enumerate(slots):
                    weights(sp, T, slot, fo(c * 2 + i))
            w_in(0, (0, 1, 2, 1))
            with sp.Fori(0, NCH // 2) as i:
                T.enter(i, w0=4, w1=4, w2=4)
                w_in(2 * i + 1)
                w_out(2 * i)
                w_in(2 * i + 2)
                w_out(2 * i + 1)
                T.leave(NCH // 2)
            w_out(NCH - 1, (0, 1))

        def proj_sp_first(sp, T, w):
            for m in range(2):
                weights(sp, T, m, w[m, :, :])

        def proj_sp(sp, T, w):
            with sp.Fori(0, KT // 2 - 1) as i:
                T.enter(i, w0=1, w1=1)
                for m in range(2):
                    weights(sp, T, m, w[2 * i + 2 + m, :, :])
                T.leave(KT // 2 - 1)

        def sync_program(sp):
            T = Tally()
            sp.dma_start(small[:, :], small_d).then_inc(s_small, 16)
            for n in range(N3):
                sp.dma_start(X[:, :, third(n)], x_t.rearrange("p (k t) -> p k t", k=KT)[:, :, third(n)]).then_inc(s_in[n], 16)

            def ab(j, first=False):
                for slot, m in ((0, 16), (1, 12), (2, 0), (0, 4), (1, 8)):
                    if first and m == 12:
                        sp.wait_ge(s_rel, 32)
                    if first and m == 0:
                        sp.wait_ge(s_const, N_CONST)
                    if first and m == 4:
                        sp.wait_ge(s_hlo, 2 * N3)
                        sp.dma_start(US[:, :, :, 0:HIST], hist_d).then_inc(s_hist, 16)
                    weights(sp, T, slot, w_ab[j + m, :, :])
            ab(0, True)
            with sp.Fori(0, AB - 1) as i:
                T.enter(i, w0=2, w1=2, w2=1)
                ab(i + 1)
                T.leave(AB - 1)
            proj_sp_first(sp, T, w_oab)
            sp.wait_ge(s_full["v"], N3 * AB)
            for b in range(NB + 1):
                if b < NB:
                    if b >= 2:
                        sp.wait_ge(s_s, b - 1)
                    sp.dma_start(KCA[:, b % 2], kc_d[b]).then_inc(s_kc[b % 2], 16)
                if b:
                    if b >= 3:
                        sp.wait_ge(s_o, b - 2)
                    sp.dma_start(VCA[:, (b - 1) % 2], vc_d[b - 1]).then_inc(s_vc[(b - 1) % 2], 16)
            sp.wait_ge(s_got["k"], N3 * AB)
            sp.dma_start(k_o, X[:, AB:KT, SEQ - CACHE:TOK]).then_inc(s_out, 16)
            sp.wait_ge(s_got["vt"], N3 * AB)
            sp.dma_start(v_o, VTOK[:, 4:NT, :]).then_inc(s_out, 16)
            sp.wait_ge(s_s, NB + AH * PT_TILES)
            sp.wait_ge(s_out, 32)
            sp.wait_ge(s_outc, 32)
            xv = x_t.rearrange("p (k t) -> p k t", k=KT)
            sp.dma_start(X[:, 0:2, :], xv[:, 0:2, :]).then_inc(s_xr[0], 16)
            sp.dma_start(X[:, 2:KT, :], xv[:, 2:KT, :]).then_inc(s_xr[1], 16)
            proj_sp(sp, T, w_oab)
            ffn_sp(sp, T, 0)
            def head(h, first=False):
                for slot, m in ((0, 8), (1, 0), (2, 16), (1, 24)):
                    weights(sp, T, slot, w_c[h + m, :, :])
                    if first and m == 16:
                        sp.wait_ge(s_x, XC_START)
                        sp.dma_start(xd, X[:, :, :].rearrange("p k t -> p (k t)")).then_inc(s_sp, 16)
            head(0, True)
            head(1)
            with sp.Fori(0, CH // 2 - 1) as i:
                T.enter(i, w0=2, w1=4, w2=2)
                head(2 * i + 2)
                head(2 * i + 3)
                T.leave(CH // 2 - 1)
            proj_sp_first(sp, T, w_oc)
            sp.wait_ge(s_hlo, H_CO)
            xdv = xd.rearrange("p (k t) -> p k t", k=KT)
            sp.dma_start(X[:, 0:2, :], xdv[:, 0:2, :]).then_inc(s_xr[0], 16)
            sp.dma_start(X[:, 2:KT, :], xdv[:, 2:KT, :]).then_inc(s_xr[1], 16)
            proj_sp(sp, T, w_oc)
            ffn_sp(sp, T, 1)
            yv = y_o.rearrange("p (k t) -> p k t", k=KT)
            for n in range(N3):
                sp.wait_ge(s_hf, HF_END - 2 * (N3 - 1 - n))
                sp.dma_start(yv[:, :, third(n)], X[:, :, third(n)]).then_inc(s_out, 16)
            sp.wait_ge(s_out, 16 * (2 + N3))
            sp.wait_ge(s_hgp, 16 * CH)
            sp.wait_ge(s_hgs, 16 * CH)

        N_CONST = 4 + 5 * LEVELS
        X_AB = N3 * KT
        XC_START = X_AB + NCH * KT * N3
        X_C = XC_START + N3 * KT
        X_END = X_C + NCH * KT * N3
        H_AB = 2 * N3
        H_ABO = H_AB + N3
        H_F0 = H_ABO + 2 * N3
        H_C = H_F0 + 2 * N3
        H_CO = H_C + 2 * N3
        H_F1 = H_CO + 2 * N3
        HF_END = 11 * N3

        def pool_program(pool):
            steps = []

            def fold_pair(base):
                for n in (1, 2):
                    pool.wait_ge(s_sq, base + 2 * (n + 1))
                    for blocks in (4, 2, 1):
                        ins = pool.tensor_tensor(SQ[:, 0:blocks, :], SQ[:, 0:blocks, :], SQ[:, blocks:2 * blocks, :], ALU.add)
                        if blocks > 1:
                            ins.then_inc(s_fold, 1)
                            steps.append(blocks)
                            pool.wait_ge(s_fold, len(steps))
                    ins.then_inc(s_ps, 1)

            rel = WR[0:AH, 1, 0:P + 257]
            pool.dma_start(rel[:, P:], rel_d).then_inc(s_rel, 16)
            pool.memset(ident[:, :], 0.0).then_inc(s_const, 1)
            pool.memset(ones[:, :], 1.0).then_inc(s_const, 1)
            pool.wait_ge(s_const, 2)
            pool.affine_select(out=ident[:, :], in_=ident[:, :], compare_op=ALU.not_equal, fill=1.0,
                               base=0, pattern=[[-1, P]], channel_multiplier=1).then_inc(s_const, 1)
            pool.iota(parity_i[:, 0:1], pattern=[[0, 1]], base=0, channel_multiplier=1).then_inc(s_const, 1)
            pool.wait_ge(s_rel, 16)
            pool.tensor_copy(rel[:, 0:P], rel[:, P:P + 1].to_broadcast([AH, P])).then_inc(s_pad, 1)
            pool.wait_ge(s_pad, 1)
            pool.dma_start(padded.ap()[:, 0:P + 257], rel).then_inc(s_rel, 16)
            pool.wait_ge(s_rel, 32)
            pool.dma_start(skewed.ap()[:, :, 0:P + 257],
                           bass.AP(tensor=padded, offset=0, ap=[[0, P], [512, AH], [1, P + 257]])).then_inc(s_rel, 16)
            fold_pair(0)
            mf = WR[:, 2, 0:P]
            n = 4
            for lv in range(LEVELS):
                w = 1 << lv
                nb = P // (2 * w)
                pool.memset(mf, 0.0).then_inc(s_const, 1)
                n += 1
                pool.wait_ge(s_const, n)
                right = mf.rearrange("p (b two w) -> p b two w", two=2, w=w)[:, :, 1, :]
                pool.memset(right, 1.0).then_inc(s_const, 1)
                n += 1
                pool.wait_ge(s_const, n)
                for base, st, cm in ((0, -2 * w, 1), (w - 1, 2 * w, -1)):
                    pool.affine_select(out=right, in_=right, compare_op=ALU.is_ge, fill=0.0, base=base,
                                       pattern=[[st, nb], [0, w]], channel_multiplier=cm).then_inc(s_const, 1)
                    n += 1
                    pool.wait_ge(s_const, n)
                pool.tensor_copy(lvl_mask[:, lv, :], mf).then_inc(s_const, 1)
                n += 1
                pool.wait_ge(s_const, n)
            pool.wait_ge(s_rel, 48)
            pool.wait_ge(s_cv, 2 * CW * AB)
            pool.wait_ge(s_co, AB)
            pool.dma_start(cvp_o, CO[:, :, :]).then_inc(s_outc, 16)
            pool.dma_start(cvs_o, US[:, :, :, NS:HIST + NS]).then_inc(s_outc, 16)
            pool.wait_ge(s_outc, 32)
            pool.wait_ge(s_full["vt"], N3 * AB)
            pitch = AH * 512 - 1
            pool.dma_start(BT[:, :, :], bass.AP(tensor=skewed, offset=P, ap=[[pitch, P], [512, AH], [1, 2 * P]])).then_inc(s_bt, 16)
            for h in range(AH):
                pool.dma_start(BS[h * NS:(h + 1) * NS, :],
                               bass.AP(tensor=skewed, offset=P + 512 * h, ap=[[pitch, NS], [1, P + NS]])).then_inc(s_bt, 16)
            for norm in range(4):
                fold_pair(2 * N3 + N3 + norm * 2 * N3)

        def cut_hi(act, T, slot, after=None):
            T.add(f"w{slot}")
            need(act, s_raw[slot], T(f"w{slot}") * 16)
            if after is not None:
                need(act, *after)
            act.activation(WH[:, slot, :], WR[:, slot, :], ACT.Copy).then_inc(s_hi, 1)

        def cut_lo(dve, T, slot):
            T.add("hi")
            need(dve, s_hi, T("hi"))
            dve.tensor_tensor(WL[:, slot, :], WR[:, slot, :], WH[:, slot, :].bitcast(F32),
                              ALU.subtract).then_inc(s_lo[slot], 1)

        def have(pe, T, slot):
            T.add(f"w{slot}")
            need(pe, s_lo[slot], T(f"w{slot}"))

        def product(out, slot, n):
            mm = None
            for k in range(KT):
                wh, wl = WH[:, slot, tile(k)], WL[:, slot, tile(k)]
                nc.tensor.matmul(out, wh, hh(k, third(n)), start=(k == 0), stop=False)
                nc.tensor.matmul(out, wh, hl(k, third(n)), start=False, stop=False)
                mm = nc.tensor.matmul(out, wl, hh(k, third(n)), start=False, stop=(k == KT - 1))
            return mm

        def norm_act(act, T, x_done, cut=None, final=False):
            def squares(n):
                if x_done is None:
                    act.wait_ge(s_in[n], 16)
                else:
                    act.wait_ge(s_x, x_done(n))
                need(act, s_ms, T("ms"))
                for half in range(2):
                    ks = slice(half * AB, (half + 1) * AB)
                    act.activation(SQ[:, ks, :], X[:, ks, third(n)], ACT.Square).then_inc(s_sq, 1)
                T.add("ms")

            def root(n):
                act.wait_ge(s_ms, T("ms"))
                act.activation(rt[:, 3 * n:3 * n + 3], PS[:, n, TH:TH + TPT], ACT.Sqrt,
                               bias=eps[:, 0:1], scale=1.0 / D).then_inc(s_rt, 1)

            def hi(n):
                if final:
                    return
                hf = HF1 if n % 2 else HF0
                for half, out in ((0, HAH), (1, HBH)):
                    T.add("hf")
                    act.wait_ge(s_hf, T("hf"))
                    act.activation(out[:, :, third(n)], hf[:, half * AB:(half + 1) * AB, :], ACT.Copy).then_inc(s_hhi, 1)
            squares(0)
            root(0)
            squares(1)
            hi(0)
            if cut:
                cut()
            root(1)
            squares(2)
            hi(1)
            root(2)
            hi(2)

        def rms_sums(pe, T, n):
            T.add("ps")
            pe.wait_ge(s_ps, T("ps"))
            for tt in range(TPT):
                mm = nc.tensor.matmul(PS[:, n, TH + tt:TH + tt + 1], SQ[:, 0, tile(tt)], ones[:, 0:1], start=True, stop=True)
            mm.then_inc(s_ms, 1)

        def rms_cast(pe, T, n):
            T.add("dg")
            pe.wait_ge(s_dg, T("dg"))
            nc.tensor.matmul(PS[:, n, 0:TH], ones[:, :], DG[:, :, :].rearrange("p a b -> p (a b)"),
                             start=True, stop=True).then_inc(s_rb, 1)

        def norm_pe(pe, T, begun=False, final=False):
            if not begun:
                rms_sums(pe, T, 0)
                rms_cast(pe, T, 0)
            rms_sums(pe, T, 1)
            rms_cast(pe, T, 1)
            if final:
                rms_sums(pe, T, 2)
                rms_cast(pe, T, 2)

        def normed(pe, T, base):
            def ready(n):
                if n == 1:
                    rms_sums(pe, T, 2)
                    rms_cast(pe, T, 2)
                pe.wait_ge(s_hlo, base + 2 * (n + 1))
            return ready

        def fold(dve, T, sq, blocks, thirds):
            T.add("sq", thirds)
            dve.wait_ge(s_sq, T("sq"))
            while blocks > 1:
                blocks //= 2
                ins = dve.tensor_tensor(sq[:, 0:blocks, :], sq[:, 0:blocks, :], sq[:, blocks:2 * blocks, :], ALU.add)
                if blocks > 1:
                    link(dve, T, ins)
            ins.then_inc(s_ps, 1)

        def rms_fold(dve, T):
            fold(dve, T, SQ, KT, 2)
            T.add("sq", 4)

        def rms_diag(dve, T, n):
            T.add("rt")
            dve.wait_ge(s_rt, T("rt"))
            need(dve, s_rb, T("rb"))
            link(dve, T, dve.reciprocal(ri[:, 3 * n:3 * n + 3], rt[:, 3 * n:3 * n + 3]))
            dve.tensor_tensor(DG[:, :, :], ident[:, :].unsqueeze(1).to_broadcast([P, TPT, P]),
                              ri[:, 3 * n:3 * n + 3].unsqueeze(2).to_broadcast([P, TPT, P]),
                              ALU.mult).then_inc(s_dg, 1)

        def rms_scale(dve, T, n, gain, final):
            T.add("rb")
            dve.wait_ge(s_rb, T("rb"))
            hf = HF1 if n % 2 else HF0
            for k in range(KT):
                out = X[:, k, third(n)] if final else hf[:, k, :]
                ins = dve.scalar_tensor_tensor(out=out, in0=X[:, k, third(n)], scalar=sm("gain", gain * KT + k),
                                               in1=PS[:, n, 0:TH], op0=ALU.mult, op1=ALU.mult)
                if k % AB == AB - 1:
                    ins.then_inc(s_hf, 1)

        def rms_lo(dve, T, n):
            hf = HF1 if n % 2 else HF0
            for half, hi, lo in ((0, HAH, HAL), (1, HBH, HBL)):
                T.add("hhi")
                dve.wait_ge(s_hhi, T("hhi"))
                dve.tensor_tensor(lo[:, :, third(n)], hf[:, half * AB:(half + 1) * AB, :],
                                  hi[:, :, third(n)].bitcast(F32), ALU.subtract).then_inc(s_hlo, 1)
                T.add("hlo")

        def norm_dve(dve, T, gain, begun=False, cut=None, final=False):
            if not begun:
                rms_fold(dve, T)
                rms_diag(dve, T, 0)
                rms_scale(dve, T, 0, gain, final)
            if not final:
                rms_lo(dve, T, 0)
            if cut:
                cut()
            rms_diag(dve, T, 1)
            rms_scale(dve, T, 1, gain, final)
            if not final:
                rms_lo(dve, T, 1)
            rms_diag(dve, T, 2)
            if not final:
                dve.wait_ge(s_hlo, T("hlo") - 2)
            rms_scale(dve, T, 2, gain, final)
            if not final:
                rms_lo(dve, T, 2)

        def link(dve, T, ins):
            T.add("dc")
            ins.then_inc(s_dc, 1)
            dve.wait_ge(s_dc, T("dc"))

        def proj_pe(pe, T, ready):
            def block(m, first):
                slot = m
                have(pe, T, slot)
                for n in range(N3):
                    if first and m == 0:
                        ready(n)
                    if not first:
                        need(pe, s_x, T("x") - 2 * N3 + 1)
                    T.add("x")
                    product(PS[:, 3 * m + n, 0:TH], slot, n).then_inc(s_xo, 1)
            block(0, True)
            block(1, True)
            with pe.Fori(0, KT // 2 - 1) as i:
                T.enter(i, w0=1, w1=1, x=2 * N3)
                block(0, False)
                block(1, False)
                T.leave(KT // 2 - 1)

        def proj_act(act, T):
            def block(m, first):
                cut_hi(act, T, 1 - m, None if first and m == 0 else (s_xo, T("x")))
                T.add("x", N3)
            block(0, True)
            block(1, True)
            with act.Fori(0, KT // 2 - 1) as i:
                T.enter(i, w0=1, w1=1, x=2 * N3)
                block(0, False)
                block(1, False)
                T.leave(KT // 2 - 1)

        def proj_dve(dve, T, reloaded):
            def block(m, blk, first):
                cut_lo(dve, T, 1 - m)
                if first and m == 0:
                    dve.wait_ge(s_xr[0], 16 * reloaded)
                for n in range(N3):
                    T.add("x")
                    need(dve, s_xo, T("x"))
                    xs = X[:, blk, third(n)]
                    dve.tensor_tensor(xs, xs, PS[:, 3 * m + n, 0:TH], ALU.add).then_inc(s_x, 1)
            block(0, 0, True)
            block(1, 1, True)
            dve.wait_ge(s_xr[1], 16 * reloaded)
            with dve.Fori(0, KT // 2 - 1) as i:
                T.enter(i, x=2 * N3, hi=2)
                block(0, i * 2 + 2, False)
                block(1, i * 2 + 3, False)
                T.leave(KT // 2 - 1)

        def output():
            for m in range(KT):
                for n in range(N3):
                    yield m, n, PS[:, 3 + (m * N3 + n + 3) % 5, 0:TH]

        def last_output():
            for n in range(N3):
                for m in range(KT):
                    yield n, m, PS[:, 3 + (KT * N3 + n * KT + m + 3) % 5, 0:TH]

        def ffn_pe(pe, T, ready):
            def w_in(first):
                sa, sb_ = ((0, 2), (1, 1)) if first else ((0, 2), (1, 0))
                for j in range(2):
                    have(pe, T, sa[j])
                    for n in range(N3):
                        if first and j == 0:
                            ready(n)
                        need(pe, s_si, T("fj") - 2)
                        T.add("fj")
                        product(PS[:, n, 0:TH], sa[j], n).then_inc(s_fa, 1)
                    have(pe, T, sb_[j])
                    if j == 0:
                        need(pe, s_x, T("x"))
                    for n in range(N3):
                        need(pe, s_u, T("fb") - 2)
                        T.add("fb")
                        product(PS[:, 3 + n, 0:TH], sb_[j], n).then_inc(s_fb, 1)

            def out_product(m, n, out, par, slots):
                T.add("x")
                for kk in range(2):
                    wh, wl = WH[:, slots[kk], tile(m)], WL[:, slots[kk], tile(m)]
                    uh, ul = UH[:, par, kk, third(n)], UL[:, par, kk, third(n)]
                    nc.tensor.matmul(out, wh, uh, start=(kk == 0), stop=False)
                    nc.tensor.matmul(out, wh, ul, start=False, stop=False)
                    mm = nc.tensor.matmul(out, wl, uh, start=False, stop=(kk == 1))
                mm.then_inc(s_xo, 1)

            def w_out(par):
                for slot in (1, 2):
                    have(pe, T, slot)
                T.add("u", 2 * N3)
                need(pe, s_ul, T("u"))
                for m, n, out in output():
                    if 2 <= m * N3 + n < 5:
                        need(pe, s_u, T("fb") - 4 + m * N3 + n)
                    need(pe, s_x, T("x") - 4)
                    out_product(m, n, out, par, (1, 2))
            w_in(True)
            with pe.Fori(0, NCH // 2) as i:
                T.enter(i, w0=4, w1=4, w2=4, fj=4 * N3, fb=4 * N3, u=4 * N3, x=2 * KT * N3)
                w_in(False)
                w_out(0)
                w_in(False)
                w_out(1)
                T.leave(NCH // 2)
            for slot in (0, 1):
                have(pe, T, slot)
            T.add("u", 2 * N3)
            for n, m, out in last_output():
                if m == 0:
                    need(pe, s_ul, T("u") - (N3 - 1) + n)
                if (n, m) == (1, 7):
                    rms_sums(pe, T, 0)
                if (n, m) == (2, 1):
                    rms_cast(pe, T, 0)
                need(pe, s_x, T("x") - 4)
                out_product(m, n, out, 0, (0, 1))

        def ffn_act(act, T):
            def w_in(par, first=False):
                for j in range(2):
                    if j == 0:
                        cut_hi(act, T, 1, (s_xo, T("x")))
                    elif first:
                        cut_hi(act, T, 1, (s_fb, T("u")))
                    else:
                        cut_hi(act, T, 0, (s_fa, T("fj")))
                    for n in range(N3):
                        T.add("fj")
                        need(act, s_fa, T("fj"))
                        need(act, s_u, T("fj") - N3)
                        act.activation(SG[:, n, :], PS[:, n, 0:TH], ACT.Silu).then_inc(s_si, 1)
                    if j == 0:
                        cut_hi(act, T, 2, (s_xo, T("x")))
                    elif first:
                        cut_hi(act, T, 0, (s_fa, T("fj")))
                    else:
                        cut_hi(act, T, 1, (s_fb, T("u")))
                        cut_hi(act, T, 2, (s_fa, T("fj")))
                    for n in range(N3):
                        T.add("u")
                        need(act, s_u, T("u"))
                        need(act, s_xo, T("x"))
                        act.activation(UH[:, par, j, third(n)], UF[:, n, :], ACT.Copy).then_inc(s_uh, 1)

            def w_out():
                cut_hi(act, T, 0, (s_fb, T("u")))
                T.add("x", KT * N3)
            w_in(0, True)
            with act.Fori(0, NCH // 2) as i:
                T.enter(i, w0=4, w1=4, w2=4, fj=4 * N3, u=4 * N3, x=2 * KT * N3)
                w_in(1)
                w_out()
                w_in(0)
                w_out()
                T.leave(NCH // 2)
            cut_hi(act, T, 1, (s_xo, T("x")))
            T.add("x", KT * N3)

        def ffn_dve(dve, T, gain, final):
            def w_in(par, first=False):
                for j in range(2):
                    cut_lo(dve, T, 1 if j == 0 or first else 0)
                    if j == 0:
                        cut_lo(dve, T, 2)
                    elif first:
                        cut_lo(dve, T, 0)
                    else:
                        cut_lo(dve, T, 1)
                        cut_lo(dve, T, 2)
                    for n in range(N3):
                        T.add("u")
                        need(dve, s_si, T("u"))
                        need(dve, s_fb, T("u"))
                        need(dve, s_uh, T("u") - N3)
                        need(dve, s_ul, T("u") - N3)
                        dve.tensor_tensor(UF[:, n, :], SG[:, n, :], PS[:, 3 + n, 0:TH], ALU.mult).then_inc(s_u, 1)
                        if n:
                            lo(par, j, n - 1, T("u") - 1)
                    lo(par, j, N3 - 1, T("u"))

            def lo(par, j, n, count):
                need(dve, s_uh, count)
                dve.tensor_tensor(UL[:, par, j, third(n)], UF[:, n, :],
                                  UH[:, par, j, third(n)].bitcast(F32), ALU.subtract).then_inc(s_ul, 1)

            def w_out():
                for m, n, out in output():
                    if (m, n) == (1, 0):
                        cut_lo(dve, T, 0)
                    T.add("x")
                    need(dve, s_xo, T("x"))
                    xs = X[:, m, third(n)]
                    dve.tensor_tensor(xs, xs, out, ALU.add).then_inc(s_x, 1)
            w_in(0, True)
            with dve.Fori(0, NCH // 2) as i:
                T.enter(i, hi=12, u=4 * N3, x=2 * KT * N3)
                w_in(1)
                w_out()
                w_in(0)
                w_out()
                T.leave(NCH // 2)
            cut_lo(dve, T, 1)
            for n, m, out in last_output():
                if (n, m) == (1, 4):
                    rms_fold(dve, T)
                if (n, m) == (2, 0):
                    rms_diag(dve, T, 0)
                if (n, m) == (2, 2):
                    rms_scale(dve, T, 0, gain, final)
                T.add("x")
                need(dve, s_xo, T("x"))
                xs = X[:, m, third(n)]
                dve.tensor_tensor(xs, xs, out, ALU.add).then_inc(s_x, 1)

        def ab_pe(pe, T):
            def step(ready=None):
                for name, slot, bank, prev, sem_prev in (
                        ("g", 0, 0, "v", s_got["v"]), ("a", 1, 3, "k", s_got["k"]), ("q", 2, 0, "g", s_got["g"]),
                        ("k", 0, 3, "a", s_got["a"]), ("v", 1, 0, "q", s_got["q"])):
                    have(pe, T, slot)
                    for n in range(N3):
                        if ready and name == "g":
                            ready(n)
                        need(pe, sem_prev, T(prev) - 2 + n)
                        product(PS[:, bank + n, 0:TH], slot, n).then_inc(s_full[name], 1)
                        if name == "v" and n:
                            turn(n - 1)
                    T.add(name, N3)
                turn(N3 - 1)
                T.add("vt", N3)

            def turn(n):
                j3 = T("vt")
                need(pe, s_got["v"], j3 + n + 1)
                need(pe, s_got["vt"], j3 + (0, -1, 1)[n])
                for tt in range(TPT):
                    mm = nc.tensor.transpose(PS[:, 6 + n % 2, tile(tt)], EV[:, n, tile(tt)], ident[:, :])
                mm.then_inc(s_full["vt"], 1)
            step(normed(pe, T, 0))
            with pe.Fori(0, AB - 1) as i:
                T.enter(i, w0=2, w1=2, w2=1, g=N3, a=N3, q=N3, k=N3, v=N3, vt=N3)
                step()
                T.leave(AB - 1)

        def ab_act(act, T):
            def token_major(j, n, three):
                need(act, s_full["vt"], three + n + 1)
                act.activation(VTOK[:, 3 * n:3 * n + 3, bass.ds(j * P, P)],
                               PS[:, 6 + n % 2, 0:TH].rearrange("p (a b) -> p a b", b=P), ACT.Copy).then_inc(s_got["vt"], 1)

            def step(j, first):
                three = T("j3")
                wait = lambda k: None if first else (s_full[k], three)
                here = lambda k: (s_full[k], three + N3)
                cut_hi(act, T, 1, wait("v"))
                for n in range(N3):
                    need(act, s_full["g"], three + n + 1)
                    need(act, s_full["vt"], three - 2 + n)
                    act.activation(EV[:, n, :], PS[:, n, 0:TH], ACT.Sigmoid).then_inc(s_got["g"], 1)
                cut_hi(act, T, 2, wait("q"))
                cut_hi(act, T, 0, here("g"))
                for n in range(N3):
                    need(act, s_full["q"], three + n + 1)
                    act.activation(X[:, j, third(n)], PS[:, n, 0:TH], ACT.Copy, scale=-AD ** -0.5).then_inc(s_got["q"], 1)
                cut_hi(act, T, 1, here("a"))
                for n in range(N3):
                    need(act, s_full["k"], three + n + 1)
                    act.activation(X[:, j + AB, third(n)], PS[:, 3 + n, 0:TH], ACT.Copy).then_inc(s_got["k"], 1)
                cut_hi(act, T, 0, here("k"))
                for n in range(N3):
                    need(act, s_full["v"], three + n + 1)
                    need(act, s_got["a"], three + n + 1)
                    act.activation(EV[:, n, :], PS[:, n, 0:TH], ACT.Copy).then_inc(s_got["v"], 1)
                    if n:
                        token_major(j, n - 1, three)
                token_major(j, N3 - 1, three)
                T.add("j3", N3)
            step(0, True)
            with act.Fori(0, AB - 1) as i:
                T.enter(i, w0=2, w1=2, w2=1, j3=N3)
                step(i + 1, False)
                T.leave(AB - 1)

        def ab_dve(dve, T):
            def conv(j, a, b):
                for t in range(a, b):
                    for part in range(2):
                        if part == 0:
                            src, out = UP[:, t:t + SEQ], Y[:, j, 0:SEQ]
                        else:
                            src = US[:, j, :, t:t + NS]
                            out = Y[:, j, SEQ:TOK].rearrange("p (b s) -> p b s", b=NB)
                        w = sm("cw", j * CW + t)
                        if t == 0:
                            ins = dve.tensor_scalar(out, src, w, sm("cb", j), ALU.mult, ALU.add)
                        else:
                            need(dve, s_cv, T("cv") - 1)
                            ins = dve.scalar_tensor_tensor(out=out, in0=src, scalar=w, in1=out, op0=ALU.mult, op1=ALU.add)
                        ins.then_inc(s_cv, 1)
                        T.add("cv")

            def step(j, first=False):
                three = T("j3")
                cut_lo(dve, T, 1)
                if not first:
                    conv(j - 1, 28, CW)
                cut_lo(dve, T, 2)
                need(dve, s_co, T("co"))
                need(dve, s_cv, T("cv"))
                for n in range(N3):
                    need(dve, s_full["a"], three + n + 1)
                    need(dve, s_got["g"], three + n + 1)
                    w = TH if n < N3 - 1 else SEQ - (N3 - 1) * TH
                    ins = dve.tensor_tensor(UP[:, HIST + n * TH:HIST + n * TH + w], EV[:, n, 0:w], PS[:, 3 + n, 0:w], ALU.mult)
                    if n == N3 - 1:
                        dve.wait_ge(s_hist, 16)
                        bs = lambda ap: ap.rearrange("p (b s) -> p b s", b=NB)
                        ins = dve.tensor_tensor(US[:, j, :, HIST:HIST + NS], bs(EV[:, n, w:TH]), bs(PS[:, 3 + n, w:TH]), ALU.mult)
                    ins.then_inc(s_got["a"], 1)
                need(dve, s_got["a"], three + N3)
                dve.tensor_copy(CO[:, j, :], UP[:, SEQ:SEQ + HIST]).then_inc(s_co, 1)
                T.add("co")
                conv(j, 0, 5)
                cut_lo(dve, T, 0)
                conv(j, 5, 14)
                cut_lo(dve, T, 1)
                conv(j, 14, 22)
                cut_lo(dve, T, 0)
                conv(j, 22, 28)
                T.add("j3", N3)
            dve.memset(UP[:, 0:HIST], 0.0).then_inc(s_dc, 1)
            T.add("dc")
            dve.wait_ge(s_dc, T("dc"))
            step(0, True)
            with dve.Fori(0, AB - 1) as i:
                T.enter(i, hi=5, j3=N3, co=1, cv=2 * CW)
                step(i + 1)
                T.leave(AB - 1)
            conv(AB - 1, 28, CW)

        def ln_pe(pe, T):
            pe.wait_ge(s_got["v"], N3 * AB)
            pe.wait_ge(s_got["q"], N3 * AB)
            for j in range(AB):
                pe.wait_ge(s_cv, 2 * CW * (j + 1))
                for n in range(N3):
                    mm = nc.tensor.matmul(PS[:, n, 0:TH], ones[:, :], Y[:, j, third(n)], start=(j == 0), stop=(j == AB - 1))
                    if j == AB - 1:
                        mm.then_inc(s_ms, 1)
            for k in ("a", "k", "vt"):
                pe.wait_ge(s_got[k], N3 * AB)
            for n in range(N3):
                T.add("ps", 1)
                pe.wait_ge(s_ps, T("ps"))
                for tt in range(TPT):
                    mm = nc.tensor.matmul(PS[:, 7, 3 * n + tt:3 * n + tt + 1], LSQ[:, 0, tile(tt)], ones[:, 0:1],
                                          start=True, stop=True)
                mm.then_inc(s_ms, 1)
                T.add("dg")
                pe.wait_ge(s_dg, T("dg"))
                nc.tensor.matmul(PS[:, 4 + n, 0:TH], ones[:, :], LDG[:, :, :].rearrange("p a b -> p (a b)"), start=True, stop=True).then_inc(s_rb, 1)

        def ln_dve(dve, T):
            dve.wait_ge(s_full["v"], N3 * AB)
            for b in range(2):
                dve.memset(QB[:, b, :, :], 0.0).then_inc(s_bias, 1)
            dve.memset(late[:, :], 0.0).then_inc(s_bias, 1)
            dve.memset(plus[:, :], -NEG).then_inc(s_bias, 1)
            dve.wait_ge(s_bias, 4)
            dve.memset(late[:, 64:P], 1.0).then_inc(s_bias, 1)
            dve.wait_ge(s_ms, T_MS + N3)
            for n in range(N3):
                for j in range(AB):
                    y = Y[:, j, third(n)]
                    ins = dve.scalar_tensor_tensor(out=y, in0=PS[:, n, 0:TH], scalar=-1.0 / AW, in1=y, op0=ALU.mult, op1=ALU.add)
                ins.then_inc(s_yc, 1)
            def diag(n):
                T.add("rt")
                dve.wait_ge(s_rt, T("rt"))
                dve.wait_ge(s_rb, T("rb"))
                link(dve, T, dve.reciprocal(ri[:, 3 * n:3 * n + 3], rt[:, 3 * n:3 * n + 3]))
                dve.tensor_tensor(LDG[:, :, :], ident[:, :].unsqueeze(1).to_broadcast([P, TPT, P]),
                                  ri[:, 3 * n:3 * n + 3].unsqueeze(2).to_broadcast([P, TPT, P]), ALU.mult).then_inc(s_dg, 1)
            fold(dve, T, LSQ, AB, 1)
            for n in range(N3):
                diag(n)
                if n < N3 - 1:
                    fold(dve, T, LSQ, AB, 1)
                T.add("rb")
                dve.wait_ge(s_rb, T("rb"))
                y = Y[:, :, third(n)]
                dve.tensor_tensor(y, y, PS[:, 4 + n, 0:TH].unsqueeze(1).to_broadcast([P, AB, TH]), ALU.mult).then_inc(s_yc, 1)

        def ln_act(act, T):
            act.wait_ge(s_outc, 32)
            T.add("ms", N3)
            for n in range(N3):
                act.wait_ge(s_yc, n + 1)
                need(act, s_ms, T("ms"))
                act.activation(LSQ[:, :, :], Y[:, :, third(n)], ACT.Square).then_inc(s_sq, 1)
                T.add("ms")
                act.wait_ge(s_ms, T("ms"))
                act.activation(rt[:, 3 * n:3 * n + 3], PS[:, 7, 3 * n:3 * n + 3], ACT.Sqrt,
                               bias=eps[:, 0:1], scale=1.0 / AW).then_inc(s_rt, 1)
            for n in range(N3):
                act.wait_ge(s_yc, N3 + n + 1)
                for j in range(AB):
                    y = Y[:, j, third(n)]
                    ins = act.activation(y, y, ACT.Silu, bias=sm("lb", j), scale=sm("lg", j))
                ins.then_inc(s_hf, 1)
                T.add("hf")

        ITEMS = NB + PT_TILES * AH

        def item(s):
            t, h = divmod(s - NB, AH)
            return t, h, min(t + 1, 5)

        def score(s, cols):
            o = (s % 2) * 1024
            return PSF[:, o + cols.start:o + cols.stop]

        def att_pe(pe, T):
            def scores(s):
                if s >= 2:
                    pe.wait_ge(s_p, s - 1)
                if s < NB:
                    pe.wait_ge(s_kc[s % 2], 16 * (s // 2 + 1))
                    pe.wait_ge(s_qb, s + 1)
                    for f in range(AB):
                        nc.tensor.matmul(score(s, slice(0, CACHE)), QB[:, s % 2, f, :], KCA[:, s % 2, f, :],
                                         start=(f == 0), stop=(f == AB - 1))
                    for f in range(AB):
                        mm = nc.tensor.matmul(score(s, slice(CACHE, CACHE + NS)), QB[:, s % 2, f, :],
                                              X[:, AB + f, SEQ + NS * s:SEQ + NS * (s + 1)],
                                              start=(f == 0), stop=(f == AB - 1))
                    mm.then_inc(s_s, 1)
                    return
                t, h, nk = item(s)
                r = slice(64 * (h % 2), 64 * (h % 2) + 64)
                q = X[r, h // 2, tile(t)]
                for lo, hi in ((5 - nk, min(4, 5)), (4, 5)):
                    if lo == hi:
                        continue
                    k0 = (t - 4 + lo) * P
                    cols = slice(lo * P, hi * P)
                    kk = X[r, AB + h // 2, k0:k0 + (hi - lo) * P]
                    cut = nk == 5 and lo == 0
                    mm = nc.tensor.matmul(score(s, cols), q, kk, start=True, stop=True)
                    if cut:
                        mm = nc.tensor.matmul(score(s, slice(0, 64)), late[:, :], plus[:, :], start=False, stop=True,
                                              skip_group_check=True)
                mm.then_inc(s_s, 1)

            def turn(s):
                pe.wait_ge(s_pn, s + 1)
                tiles = range(5 if s < NB else item(s)[2])
                tiles = range(5 - len(tiles), 5)
                need(pe, s_ptc, s)
                for c in tiles:
                    mm = nc.tensor.transpose(PSF[:, 2048 + c * P:2048 + (c + 1) * P], PR[:, s % 2, tile(c)], ident[:, :])
                mm.then_inc(s_pt, 1)

            def values(s):
                pe.wait_ge(s_ptc, s + 1)
                if s < NB:
                    pe.wait_ge(s_vc[s % 2], 16 * (s // 2 + 1))
                    need(pe, s_os, s)
                    for c in range(5):
                        v = VCA[:, s % 2, c, :] if c < 4 else VTOK[:, NT - 1, :]
                        mm = nc.tensor.matmul(PS[:, 6, :], PRT[:, s % 2, tile(c)], v, start=(c == 0), stop=(c == 4))
                    mm.then_inc(s_o, 1)
                    return
                t, h, nk = item(s)
                if h == 0:
                    pe.wait_ge(s_alo, 2 * NB + max(t - 1, 0))
                for c in range(5 - nk, 5):
                    mm = nc.tensor.matmul(PS[64 * (h % 2):64 * (h % 2) + 64, 6 + t % 2, tile(h // 2)],
                                          VTOK[:, t - 4 + c, h * AD:(h + 1) * AD], PRT[:, s % 2, tile(c)],
                                          start=(c == 5 - nk), stop=(c == 4))
                mm.then_inc(s_o, 1)

            def stream_turn(b):
                pe.wait_ge(s_os, b + 1)
                need(pe, s_alo, 2 * b)
                for f in range(AB):
                    mm = nc.tensor.transpose(PS[:, 7, tile(f)], OS[:, tile(f)], ident[:, :])
                mm.then_inc(s_ot, 1)

            pe.wait_ge(s_got["k"], N3 * AB)
            pe.wait_ge(s_got["q"], N3 * AB)
            pe.wait_ge(s_got["vt"], N3 * AB)
            pe.wait_ge(s_got["a"], N3 * AB)
            scores(0)
            for s in range(ITEMS + 1):
                if s + 1 < ITEMS:
                    scores(s + 1)
                if s:
                    values(s - 1)
                if s < ITEMS:
                    turn(s)
                if 1 <= s <= NB:
                    stream_turn(s - 1)

        def att_act(act, T):
            def probs(s):
                act.wait_ge(s_nm, s + 1)
                if s >= 2:
                    act.wait_ge(s_pt, s - 1)
                if s < NB:
                    act.activation(PR[:, s % 2, 0:CACHE], score(s, slice(0, CACHE)), ACT.Exp, scale=-1.0, bias=nmax[:, s % 2:s % 2 + 1],
                                   accum_out=psum_[:, 0 + 2 * (s % 2):1 + 2 * (s % 2)])
                    act.activation(PR[:, s % 2, CACHE + NS * s:CACHE + NS * (s + 1)], score(s, slice(CACHE, CACHE + NS)), ACT.Exp, scale=-1.0,
                                   bias=nmax[:, s % 2:s % 2 + 1],
                                   accum_out=psum_[:, 1 + 2 * (s % 2):2 + 2 * (s % 2)]).then_inc(s_p, 1)
                    return
                t, h, nk = item(s)
                cols = slice((5 - nk) * P, 5 * P)
                act.activation(PR[:, s % 2, cols], score(s, cols), ACT.Exp, scale=-1.0, bias=nmax[:, s % 2:s % 2 + 1],
                               accum_out=psum_[:, 2 * (s % 2):2 * (s % 2) + 1]).then_inc(s_p, 1)

            def scaled(s):
                act.wait_ge(s_rs, s + 1)
                cols = slice(0, 5 * P) if s < NB else slice((5 - item(s)[2]) * P, 5 * P)
                act.activation(PR[:, s % 2, cols], PR[:, s % 2, cols], ACT.Copy, scale=rsum[:, 1:2]).then_inc(s_pn, 1)

            def turned(s):
                act.wait_ge(s_pt, s + 1)
                if s >= 2:
                    act.wait_ge(s_o, s - 1)
                nk = 5 if s < NB else item(s)[2]
                cols = slice((5 - nk) * P, 5 * P)
                act.activation(PRT[:, s % 2, cols], PSF[:, 2048 + cols.start:2048 + cols.stop], ACT.Copy).then_inc(s_ptc, 1)

            def stream_rows(b):
                act.wait_ge(s_o, b + 1)
                need(act, s_ot, b)
                act.activation(OS[:, :], PS[:, 6, :], ACT.Copy).then_inc(s_os, 1)

            def stream_hi(b):
                act.wait_ge(s_ot, b + 1)
                for half in range(2):
                    act.activation(stream_part(HAH, b, half), stream_out(half), ACT.Copy).then_inc(s_ahi, 1)

            def rows(t):
                act.wait_ge(s_o, NB + AH * (t + 1))
                act.activation(HAH[:, :, tile(t)], PS[:, 6 + t % 2, :].rearrange("p (f n) -> p f n", f=AB), ACT.Copy).then_inc(s_ahi, 1)
            for s in range(ITEMS + 1):
                if s < ITEMS:
                    probs(s)
                if 1 <= s <= ITEMS:
                    turned(s - 1)
                if 2 <= s < NB + 2:
                    stream_hi(s - 2)
                for n in range(N3):
                    if s == NB + 4 + 2 * n:
                        act.activation(HBH[:, :, third(n)], Y[:, :, third(n)], ACT.Copy).then_inc(s_hhi, 1)
                if s >= NB + AH + 2 and (s - 2) % AH == 0:
                    rows((s - 2 - NB) // AH - 1)
                if s < ITEMS:
                    scaled(s)
                if 1 <= s <= NB:
                    stream_rows(s - 1)
            rows(PT_TILES - 1)

        def stream_out(half):
            rows = PS[64 * half:64 * half + 64, 7, half * NS:half * NS + (AB - 1) * (P + 2 * NS) + NS]
            return bass.AP(tensor=rows.tensor, offset=rows.offset, ap=[list(rows.ap[0]), [P + 2 * NS, AB], [1, NS]])

        def stream_part(part, b, half):
            return part[64 * half:64 * half + 64, :, SEQ + NS * b:SEQ + NS * (b + 1)]

        def att_dve(dve, T):
            dve.wait_ge(s_bt, 16 * (1 + AH))
            link(dve, T, dve.tensor_copy(rt[:, 8:9], BS[:, 0:1]))
            dve.tensor_scalar(BS[:, :], BS[:, :], rt[:, 8:9], None, ALU.subtract).then_inc(s_bias, 1)
            for b in range(2):
                dve.memset(PR[:, b, CACHE:5 * P], 0.0).then_inc(s_bias, 1)
            dve.wait_ge(s_bias, 8)

            def tables():
                link(dve, T, dve.tensor_copy(rt[:, 0:AH], BT[:, :, 0]))
                link(dve, T, dve.tensor_tensor(BT[:, :, :], BT[:, :, :], rt[:, 0:AH].unsqueeze(2).to_broadcast([P, AH, 2 * P]),
                                               ALU.subtract))
                link(dve, T, dve.tensor_scalar(BT[0:64, :, P + 64:2 * P], BT[0:64, :, P + 64:2 * P], NEG, None, ALU.add))

            def queries(s):
                if s >= 2:
                    dve.wait_ge(s_s, s - 1)
                for half in range(2):
                    r = slice(64 * half, 64 * half + 64)
                    out = CACHES[r, 8192 + (s % 2) * 512 + half * NS:8192 + (s % 2) * 512 + half * NS + 3 * (P + 2 * NS) + NS]
                    out = bass.AP(tensor=out.tensor, offset=out.offset,
                                  ap=[list(out.ap[0]), [P + 2 * NS, AB], [1, NS]])
                    ins = dve.tensor_copy(out, X[r, 0:AB, SEQ + NS * s:SEQ + NS * (s + 1)])
                ins.then_inc(s_qb, 1)

            def maximum(s):
                dve.wait_ge(s_s, s + 1)
                if s >= 2:
                    dve.wait_ge(s_p, s - 1)
                if s < NB:
                    near, table, cols = slice(CACHE - P, CACHE + NS), BS[:, :], slice(0, CACHE + NS)
                else:
                    t, h, nk = item(s)
                    nn = min(nk, 2)
                    near, table = slice((5 - nn) * P, 5 * P), BT[:, h, (2 - nn) * P:2 * P]
                    cols = slice((5 - nk) * P, 5 * P)
                link(dve, T, dve.tensor_tensor(score(s, near), score(s, near), table, ALU.subtract))
                dve.tensor_reduce(nmax[:, s % 2:s % 2 + 1], score(s, cols), AX.X, ALU.min).then_inc(s_nm, 1)

            def normalise(s):
                o = 2 * (s % 2)
                dve.wait_ge(s_p, s + 1)
                need(dve, s_pn, s)
                total = psum_[:, o:o + 1]
                if s < NB:
                    if s >= 2:
                        link(dve, T, dve.memset(PR[:, s % 2, CACHE + NS * (s - 2):CACHE + NS * (s - 1)], 0.0))
                    link(dve, T, dve.tensor_tensor(rsum[:, 0:1], total, psum_[:, o + 1:o + 2], ALU.add))
                    total = rsum[:, 0:1]
                dve.reciprocal(rsum[:, 1:2], total).then_inc(s_rs, 1)

            def rows(t):
                dve.wait_ge(s_ahi, 2 * NB + t + 1)
                dve.tensor_tensor(HAL[:, :, tile(t)], PS[:, 6 + t % 2, :].rearrange("p (f n) -> p f n", f=AB),
                                  HAH[:, :, tile(t)].bitcast(F32), ALU.subtract).then_inc(s_alo, 1)

            def stream_lo(b):
                dve.wait_ge(s_ahi, 2 * (b + 1))
                for half in range(2):
                    dve.tensor_tensor(stream_part(HAL, b, half), stream_out(half),
                                      stream_part(HAH, b, half).bitcast(F32), ALU.subtract).then_inc(s_alo, 1)
            queries(0)
            for s in range(ITEMS + 2):
                if s + 1 < NB:
                    queries(s + 1)
                if s == 3:
                    tables()
                if 1 <= s <= ITEMS:
                    normalise(s - 1)
                if s < ITEMS:
                    maximum(s)
                if 2 <= s < NB + 2:
                    stream_lo(s - 2)
                for n in range(N3):
                    if s == NB + 4 + 2 * n:
                        T.add("hhi")
                        dve.wait_ge(s_hhi, T("hhi"))
                        dve.tensor_tensor(HBL[:, :, third(n)], Y[:, :, third(n)], HBH[:, :, third(n)].bitcast(F32),
                                          ALU.subtract).then_inc(s_hlo, 1)
                        T.add("hlo")
                if s >= NB + AH + 2 and (s - 2) % AH == 0:
                    rows((s - 2 - NB) // AH - 1)
            rows(PT_TILES - 1)

        C_ORDER = [(k, n) for k in "fqvg" for n in range(N3)]
        C_SLOT = dict(f=0, q=1, v=2, g=1)
        C_LAST = {(k, n): C_ORDER[i - 2] for i, (k, n) in enumerate(C_ORDER)}

        def level_tiles(lv, n):
            hi = NT if lv <= SLEVELS else PT_TILES
            return range(TPT * n, min(TPT * n + TPT, hi))

        def state_bank(b):
            return PS[:, 6 + b // 2 % 2, tile(2 * (b // 4) + b % 2)]

        def c_pe(pe, T):
            def proj(k, n, p, ready):
                if n == 0:
                    have(pe, T, C_SLOT[k])
                if ready and k == "f":
                    ready(n)
                lk, ln = C_LAST[(k, n)]
                done = T("head") * N3 + ln + 1 - (N3 if (lk, k) == ("g", "f") else 0)
                need(pe, s_cg[lk], done)
                product(PS[:, (C_ORDER.index((k, n))) % 2, 0:TH], C_SLOT[k], n).then_inc(s_cf[k], 1)

            def vturn(n, p):
                need(pe, s_cg["v"], T("head") * N3 + n + 1)
                need(pe, s_vk, T("vk"))
                T.add("vk")
                if n == 0:
                    need(pe, s_cr, T("hgrn"))
                for tt in range(TPT):
                    mm = nc.tensor.transpose(PS[:, 2, tile(tt)], VT[:, n, tile(tt)], ident[:, :])
                mm.then_inc(s_vt, 1)

            def level(lv, p):
                T.add("up")
                need(pe, s_up, T("up"))
                for n in range(N3):
                    if lv == 0:
                        need(pe, s_cn, T("hgrn") * N3)
                    else:
                        need(pe, s_mg, T("mg") - 2)
                    T.add("mg")
                    for t in level_tiles(lv, n):
                        mm = nc.tensor.matmul(PS[:, 3 + n, tile(t % TPT)], KC[:, tile(t)], QC[:, p, tile(t)],
                                              start=True, stop=True)
                    mm.then_inc(s_lv, 1)

            def kturn(n):
                T.add("kt")
                need(pe, s_up, T("up") + 1)
                need(pe, s_mg, T("mg") - 2 + n)
                for tt in range(TPT):
                    mm = nc.tensor.transpose(PS[:, 3 + n, tile(tt)], KC[:, tile(TPT * n + tt)], ident[:, :])
                mm.then_inc(s_kt, 1)

            def states(p):
                need(pe, s_kd, T("kt"))
                need(pe, s_sn, T("hgrn") * NB)
                for c in range(PT_TILES):
                    mm = nc.tensor.matmul(PS[:, 6 + c // 4, tile(c % 4)], KD[:, c, :], VC[:, p, c, :], start=True, stop=True)
                mm.then_inc(s_st, 1)

            def sample_states():
                need(pe, s_ss, T("hgrn") * PT_TILES + PT_TILES)
                need(pe, s_vm, T("hgrn") + 1)
                for b in range(NB):
                    if b == NB // 2:
                        T.add("sf")
                        mm.then_inc(s_sf, 1)
                        need(pe, s_sf, T("sf"))
                    r = slice(32 * (b // 2), 32 * (b // 2) + 32)
                    mm = nc.tensor.matmul(state_bank(b), KD[r, NT - 1, :], VM[r, b % 2, :], start=True, stop=True)
                mm.then_inc(s_sm, 1)

            def outputs(n, p):
                if n == 0:
                    need(pe, s_mg, T("mg"))
                    need(pe, s_ss, (T("hgrn") + 1) * PT_TILES)
                    need(pe, s_s0, (T("hgrn") + 1) * 16)
                for t in range(TPT * n, TPT * n + TPT):
                    out = PS[:, 3 + n, tile(t % TPT)]
                    mm = nc.tensor.matmul(out, VC[:, p, t, :], AM[:, t, :], start=True, stop=(t in (0, PT_TILES)))
                    if 0 < t < PT_TILES:
                        mm = nc.tensor.matmul(out, SS[:, t - 1, :], QC[:, p, tile(t)], start=False, stop=True)
                    if t == PT_TILES:
                        for b in range(NB):
                            mm = nc.tensor.matmul(out[:, NS * b:NS * (b + 1)], S0[:, b, :],
                                                  QC[:, p, SEQ + NS * b:SEQ + NS * (b + 1)], start=False, stop=True,
                                                  skip_group_check=True)
                mm.then_inc(s_oc, 1)

            def norm_sums():
                need(pe, s_oq, T("hgrn") * N3 + N3)
                need(pe, s_vk, T("vk"))
                for t in range(NT):
                    mm = nc.tensor.matmul(PS[:, 2, TH + t:TH + t + 1], AM[:, t, :], ones[:, 0:1], start=True, stop=True)
                mm.then_inc(s_cm, 1)

            def norm_cast():
                need(pe, s_cd, T("hgrn") + 1)
                need(pe, s_og, T("hgrn") * N3 + N3)
                for n in range(N3):
                    mm = nc.tensor.matmul(PS[:, 3 + n, 0:TH], ones[:, :],
                                          KD[:, TPT * n:TPT * n + TPT, :].rearrange("p a b -> p (a b)"), start=True, stop=True)
                    mm.then_inc(s_cb, 1)

            def step(pp, hp, ready=None):
                for i, (k, n) in enumerate(C_ORDER):
                    if pp is not None:
                        proj(k, n, pp, ready)
                        if k == "v" and n:
                            vturn(n - 1, pp)
                        if k == "g" and n == 0:
                            vturn(N3 - 1, pp)
                    if hp is None:
                        continue
                    if i <= LEVELS:
                        level(i, hp)
                    if i == 8:
                        for m in range(N3):
                            kturn(m)
                        states(hp)
                    if i == 9:
                        for m in range(N3):
                            outputs(m, hp)
                        sample_states()
                    if i == 10:
                        norm_sums()
                    if i == 11:
                        norm_cast()
                if pp is not None:
                    T.add("head")
                if hp is not None:
                    T.add("up")
                    T.add("hgrn")
            step(0, None, normed(pe, T, H_F0))
            step(1, 0)
            with pe.Fori(0, CH // 2 - 1) as i:
                T.enter(i, w0=2, w1=4, w2=2, up=2 * (LEVELS + 2), mg=2 * N3 * (LEVELS + 1), kt=2 * N3, vk=2 * N3, head=2, hgrn=2, sf=2)
                step(0, 1)
                step(1, 0)
                T.leave(CH // 2 - 1)
            step(None, 1)

        def c_act(act, T):
            def take(k, n, p, h):
                count = T("head") * N3 + n + 1
                if n == 0:
                    slot, last = {"f": (1, "g"), "q": (2, "v"), "v": (1, "q"), "g": (0, "f")}[k]
                    prev = T("head") * N3 + (0 if k in "fq" else N3)
                    cut_hi(act, T, slot, (s_cf[last], prev))
                if k == "g" and n == 0 and T.i is None and T("head") == 0:
                    act.wait_ge(s_sp, 16)
                need(act, s_cf[k], count)
                src = PS[:, C_ORDER.index((k, n)) % 2, 0:TH]
                if k == "f":
                    if n == 0:
                        need(act, s_mg, (T("head") - 1) * N3 * (LEVELS + 1))
                    act.activation(FG[:, p, third(n)], src, ACT.Sigmoid).then_inc(s_cg[k], 1)
                elif k == "q":
                    if n == 0:
                        need(act, s_oc, (T("head") - 1) * N3)
                    act.activation(QC[:, p, third(n)], src, ACT.Copy).then_inc(s_cg[k], 1)
                elif k == "v":
                    need(act, s_vt, count - N3)
                    act.activation(VT[:, n, :], src, ACT.Copy).then_inc(s_cg[k], 1)
                else:
                    act.activation(X[:, h, third(n)], src, ACT.Sigmoid).then_inc(s_gs, 1)

            def vtake(n, p):
                need(act, s_vt, T("head") * N3 + n + 1)
                if n == 0:
                    need(act, s_vm, T("head") - 1)
                act.activation(VC[:, p, TPT * n:TPT * n + TPT, :], PS[:, 2, 0:TH].rearrange("p (a b) -> p a b", b=P),
                               ACT.Copy).then_inc(s_vk, 1)

            def ktake(n):
                need(act, s_kt, T("hgrn") * N3 + n + 1)
                act.activation(KD[:, TPT * n:TPT * n + TPT, :], PS[:, 3 + n, 0:TH].rearrange("p (a b) -> p a b", b=P),
                               ACT.Copy).then_inc(s_kd, 1)

            def square(n):
                need(act, s_oc, T("hgrn") * N3 + n + 1)
                act.activation(AM[:, TPT * n:TPT * n + TPT, :], PS[:, 3 + n, 0:TH].rearrange("p (a b) -> p a b", b=P),
                               ACT.Square).then_inc(s_oq, 1)

            def root():
                need(act, s_cm, T("hgrn") + 1)
                act.activation(rt[:, 0:NT], PS[:, 2, TH:TH + NT], ACT.Sqrt, bias=eps[:, 0:1], scale=1.0 / P).then_inc(s_cr, 1)

            def load_state(h):
                need(act, s_hgs, T("hgrn") * 16)
                act.dma_start(S0[:, :, :], state_d[h]).then_inc(s_s0, 16)

            def store_states(h):
                need(act, s_ss, (T("hgrn") + 1) * PT_TILES)
                act.dma_start(hgp_o[h], SS[:, PT_TILES - 1, :]).then_inc(s_hgp, 16)
                need(act, s_sn, (T("hgrn") + 1) * NB)
                act.dma_start(hgs_o[h], S0[:, :, :]).then_inc(s_hgs, 16)

            def step(pp, hp, h):
                for i, (k, n) in enumerate(C_ORDER):
                    if hp is not None and i == 2:
                        load_state(h - 1)
                    if pp is not None:
                        take(k, n, pp, h)
                        if k == "v" and n:
                            vtake(n - 1, pp)
                        if k == "g" and n == 0:
                            vtake(N3 - 1, pp)
                    if hp is None:
                        continue
                    if i == 8:
                        for m in range(N3):
                            ktake(m)
                    if i == 9:
                        for m in range(N3):
                            square(m)
                    if i == 10:
                        root()
                    if i == 11:
                        store_states(h - 1)
                if pp is not None:
                    T.add("head")
                if hp is not None:
                    T.add("hgrn")
            step(0, None, 0)
            step(1, 0, 1)
            with act.Fori(0, CH // 2 - 1) as i:
                T.enter(i, w0=2, w1=4, w2=2, head=2, hgrn=2)
                step(0, 1, 2 * i + 2)
                step(1, 0, 2 * i + 3)
                T.leave(CH // 2 - 1)
            step(None, 1, CH)

        def c_dve(dve, T):
            def gate(n, h):
                T.add("gs")
                need(dve, s_gs, T("gs"))
                o = X[:, h, third(n)]
                dve.tensor_tensor(o, o, PS[:, C_ORDER.index(("g", n)) % 2, 0:TH], ALU.mult).then_inc(s_cg["g"], 1)

            def start(p, h):
                need(dve, s_cg["f"], (T("hgrn") + 1) * N3)
                need(dve, s_cg["q"], (T("hgrn") + 1) * N3)
                need(dve, s_kt, T("hgrn") * N3)
                link(dve, T, dve.tensor_scalar(FG[:, p, :], FG[:, p, :], low[:, 5, bass.ds(h, 1)], low[:, 4, bass.ds(h, 1)],
                                               ALU.mult, ALU.add))
                dve.tensor_scalar(KC[:, :], FG[:, p, :], -1.0, 1.0, ALU.mult, ALU.add).then_inc(s_up, 1)

            def totals(lv):
                return TA if lv % 2 else TB

            def level(lv, p):
                T.add("lv", N3)
                need(dve, s_lv, T("lv"))
                if lv == 0:
                    q = QC[:, p, :]
                    dve.tensor_tensor(q, q, FG[:, p, :], ALU.mult).then_inc(s_up, 1)
                else:
                    cols = TOK if lv <= SLEVELS else SEQ
                    w = 1 << (lv - 1)
                    nb = cols // (2 * w)
                    two = lambda ap: ap.rearrange("p (b two w) -> p b two w", two=2, w=w)
                    src = (FG[:, p, 0:cols] if lv == 1 else totals(lv - 1)[:, 0:cols // w])
                    pair = src.rearrange("p (b two) -> p b two", two=2)
                    qv, kv = two(QC[:, p, 0:cols]), two(KC[:, 0:cols])
                    dve.tensor_tensor(qv[:, :, 1, :], qv[:, :, 1, :], pair[:, :, 0].unsqueeze(2).to_broadcast([P, nb, w]), ALU.mult)
                    dve.tensor_tensor(kv[:, :, 0, :], kv[:, :, 0, :], pair[:, :, 1].unsqueeze(2).to_broadcast([P, nb, w]),
                                      ALU.mult).then_inc(s_up, 1)
                for n in range(N3):
                    tiles = level_tiles(lv, n)
                    nt = len(tiles)
                    a = AM[:, tiles.start:tiles.stop, :]
                    ps = PS[:, 3 + n, 0:nt * P].rearrange("p (a b) -> p a b", b=P)
                    if lv == 0:
                        ins = dve.tensor_tensor(a, ps, ident[:, :].unsqueeze(1).to_broadcast([P, nt, P]), ALU.mult)
                    else:
                        ins = dve.copy_predicated(a, lvl_mask[:, lv - 1, :].unsqueeze(1).to_broadcast([P, nt, P]), ps)
                    ins.then_inc(s_mg, 1)
                    T.add("mg")
                if lv:
                    out = TS[:, NB:2 * NB] if lv == LEVELS else totals(lv)[:, 0:nb]
                    ins = dve.tensor_tensor(out, pair[:, :, 0], pair[:, :, 1], ALU.mult)
                    if lv == SLEVELS:
                        link(dve, T, ins)
                        ins = dve.tensor_copy(TS[:, 0:NB], out[:, SEQ // NS:TOK // NS])
                    link(dve, T, ins)

            def mask_values(p):
                need(dve, s_vk, (T("hgrn") + 1) * N3)
                for e in range(2):
                    ins = dve.tensor_scalar(VM[:, e, :], VC[:, p, NT - 1, :], parity[:, e:e + 1], None, ALU.mult)
                ins.then_inc(s_vm, 1)

            def states():
                need(dve, s_st, T("hgrn") + 1)
                need(dve, s_hgp, T("hgrn") * 16)
                for c in range(PT_TILES):
                    ps = PS[:, 6 + c // 4, tile(c % 4)]
                    if c == 0:
                        ins = dve.tensor_copy(SS[:, 0, :], ps)
                    else:
                        need(dve, s_ss, T("ss"))
                        ins = dve.scalar_tensor_tensor(out=SS[:, c, :], in0=SS[:, c - 1, :], scalar=TS[:, NB + c:NB + c + 1],
                                                       in1=ps, op0=ALU.mult, op1=ALU.add)
                    ins.then_inc(s_ss, 1)
                    T.add("ss")

            def gated(n, h):
                need(dve, s_oc, T("hgrn") * N3 + n + 1)
                need(dve, s_oq, T("hgrn") * N3 + n + 1)
                o = X[:, h, third(n)]
                dve.tensor_tensor(o, o, PS[:, 3 + n, 0:TH], ALU.mult).then_inc(s_og, 1)

            def sample_states():
                need(dve, s_sm, T("hgrn") + 1)
                for b in range(NB):
                    dve.scalar_tensor_tensor(out=S0[:, b, :], in0=S0[:, b, :], scalar=TS[:, b:b + 1],
                                             in1=state_bank(b), op0=ALU.mult, op1=ALU.add).then_inc(s_sn, 1)

            def diagonal():
                need(dve, s_cr, T("hgrn") + 1)
                link(dve, T, dve.reciprocal(ri[:, 0:NT], rt[:, 0:NT]))
                dve.tensor_tensor(KD[:, :, :], ident[:, :].unsqueeze(1).to_broadcast([P, NT, P]),
                                  ri[:, 0:NT].unsqueeze(2).to_broadcast([P, NT, P]), ALU.mult).then_inc(s_cd, 1)

            def finish(h):
                for n in range(N3):
                    need(dve, s_cb, T("hgrn") * N3 + n + 1)
                    o = X[:, h, third(n)]
                    dve.scalar_tensor_tensor(out=o, in0=o, scalar=sm("gn"), in1=PS[:, 3 + n, 0:TH], op0=ALU.mult,
                                             op1=ALU.mult).then_inc(s_cn, 1)

            def step(pp, hp, h):
                if hp is not None:
                    start(hp, h - 1)
                for i, (k, n) in enumerate(C_ORDER):
                    if pp is not None and n == 0:
                        cut_lo(dve, T, {"f": 1, "q": 2, "v": 1, "g": 0}[k])
                    if hp is not None:
                        if i <= LEVELS:
                            level(i, hp)
                        if i == 8:
                            mask_values(hp)
                            states()
                        if i == 9:
                            for m in range(N3):
                                gated(m, h - 1)
                            sample_states()
                        if i == 11:
                            diagonal()
                    if pp is not None and k == "g":
                        gate(n, h)
                if hp is not None:
                    finish(h - 1)
                    T.add("hgrn")
            step(0, None, 0)
            step(1, 0, 1)
            with dve.Fori(0, CH // 2 - 1) as i:
                T.enter(i, hi=8, gs=2 * N3, dc=2 * (1 + LEVELS + 1 + 1), lv=2 * N3 * (LEVELS + 1), mg=2 * N3 * (LEVELS + 1),
                        ss=2 * PT_TILES, hgrn=2)
                step(0, 1, 2 * i + 2)
                step(1, 0, 2 * i + 3)
                T.leave(CH // 2 - 1)
            step(None, 1, CH)

        def cut_o_act(act, T):
            act.wait_ge(s_cf["g"], N3 * CH)
            act.wait_ge(s_cn, N3 * CH)
            for n in range(N3):
                for half, hi in ((0, HAH), (1, HBH)):
                    act.activation(hi[:, :, third(n)], X[:, half * AB:(half + 1) * AB, third(n)], ACT.Copy).then_inc(s_hhi, 1)

        def cut_o_dve(dve, T):
            for n in range(N3):
                for half, hi, lo in ((0, HAH, HAL), (1, HBH, HBL)):
                    T.add("hhi")
                    dve.wait_ge(s_hhi, T("hhi"))
                    dve.tensor_tensor(lo[:, :, third(n)], X[:, half * AB:(half + 1) * AB, third(n)],
                                      hi[:, :, third(n)].bitcast(F32), ALU.subtract).then_inc(s_hlo, 1)
                    T.add("hlo")

        s_gs = sem("s_gs")
        s_low = sem("s_low")
        s_lowe = sem("s_lowe")
        T_MS = N3

        block = ctx.enter_context(nc.Block())

        @block.sync
        def _(sp):
            sync_program(sp)

        @block.gpsimd
        def _(pool):
            pool_program(pool)

        @block.tensor
        def _(pe):
            T = Tally()
            pe.wait_ge(s_const, 3)
            norm_pe(pe, T)
            ab_pe(pe, T)
            ln_pe(pe, T)
            att_pe(pe, T)

            def both(n):
                pe.wait_ge(s_hlo, H_AB + n + 1)
                pe.wait_ge(s_alo, 2 * NB + min(TPT * (n + 1), PT_TILES))
            proj_pe(pe, T, both)
            norm_pe(pe, T)
            ffn_pe(pe, T, normed(pe, T, H_ABO))
            norm_pe(pe, T, begun=True)
            c_pe(pe, T)
            proj_pe(pe, T, lambda n: pe.wait_ge(s_hlo, H_C + 2 * (n + 1)))
            norm_pe(pe, T)
            ffn_pe(pe, T, normed(pe, T, H_CO))
            norm_pe(pe, T, begun=True, final=True)

        @block.scalar
        def _(act):
            T = Tally()
            act.wait_ge(s_small, 16)
            act.wait_ge(s_low, 3)
            act.activation(low[:, 0:2, :], low[:, 0:2, :], ACT.Exp).then_inc(s_lowe, 1)
            norm_act(act, T, None, lambda: cut_hi(act, T, 0))
            act.wait_ge(s_hlo, 2 * N3)
            ab_act(act, T)
            ln_act(act, T)
            att_act(act, T)
            proj_act(act, T)
            norm_act(act, T, lambda n: X_AB - N3 + n + 1)
            act.wait_ge(s_hlo, H_F0)
            ffn_act(act, T)
            norm_act(act, T, lambda n: XC_START - KT * (N3 - 1 - n), lambda: cut_hi(act, T, 0, (s_xo, T("x"))))
            act.wait_ge(s_hlo, H_C - 2)
            c_act(act, T)
            cut_o_act(act, T)
            proj_act(act, T)
            act.wait_ge(s_hgp, 16 * CH)
            act.wait_ge(s_hgs, 16 * CH)
            norm_act(act, T, lambda n: X_C - N3 + n + 1)
            act.wait_ge(s_hlo, H_F1)
            ffn_act(act, T)
            norm_act(act, T, lambda n: X_END - KT * (N3 - 1 - n), final=True)

        @block.vector
        def _(dve):
            T = Tally()
            dve.memset(eps[:, :], EPS).then_inc(s_low, 1)
            dve.wait_ge(s_small, 16)
            dve.wait_ge(s_const, 4)
            link(dve, T, dve.tensor_scalar(parity_i[:, 1:2], parity_i[:, 0:1], 4, 1, ALU.logical_shift_right, ALU.bitwise_and))
            link(dve, T, dve.tensor_copy(parity[:, 1:2], parity_i[:, 1:2]))
            link(dve, T, dve.tensor_scalar(parity[:, 0:1], parity[:, 1:2], -1.0, 1.0, ALU.mult, ALU.add))
            l0, l1 = sm("low", 0, CH), sm("low", CH, CH)
            link(dve, T, dve.tensor_tensor(low[:, 2, :], l0, l1, ALU.max))
            dve.tensor_tensor(low[:, 0, :], l0, low[:, 2, :], ALU.subtract).then_inc(s_low, 1)
            dve.tensor_tensor(low[:, 1, :], l1, low[:, 2, :], ALU.subtract).then_inc(s_low, 1)
            dve.wait_ge(s_lowe, 1)
            link(dve, T, dve.tensor_tensor(low[:, 3, :], low[:, 0, :], low[:, 1, :], ALU.add))
            link(dve, T, dve.reciprocal(low[:, 2, :], low[:, 3, :]))
            link(dve, T, dve.tensor_tensor(low[:, 4, :], low[:, 1, :], low[:, 2, :], ALU.mult))
            link(dve, T, dve.tensor_scalar(low[:, 5, :], low[:, 4, :], -1.0, 1.0, ALU.mult, ALU.add))
            norm_dve(dve, T, 0, cut=lambda: cut_lo(dve, T, 0))
            ab_dve(dve, T)
            ln_dve(dve, T)
            att_dve(dve, T)
            proj_dve(dve, T, 1)
            norm_dve(dve, T, 2)
            ffn_dve(dve, T, 1, False)
            norm_dve(dve, T, 1, begun=True, cut=lambda: cut_lo(dve, T, 0))
            c_dve(dve, T)
            cut_o_dve(dve, T)
            proj_dve(dve, T, 2)
            norm_dve(dve, T, 3)
            ffn_dve(dve, T, 4, True)
            norm_dve(dve, T, 4, begun=True, final=True)


def kernel(x_prompt, x_sample, cache_a_k, cache_a_v, state_conv, state_hgrn, attn_norm, ffn_norm, final_norm,
           w_in_ab, rel_bias, conv_w, conv_b, conv_ln_g, conv_ln_b, w_out_ab, w_in_c, lower_bounds, c_norm_g,
           w_out_c, ffn_w_in, ffn_w_out):
    import numpy as np
    import concourse.bacc as bacc
    from concourse.bass_utils import run_bass_kernel_spmd

    a = np.asarray
    x = np.concatenate([a(x_prompt).reshape(SEQ, D), a(x_sample).reshape(NB * NS, D)])
    by_block = lambda v: a(v).reshape(-1, P).T
    tiles = lambda w: a(w).reshape(KT, P, -1, P).transpose(2, 1, 0, 3).reshape(-1, P, D)
    fi = a(ffn_w_in).reshape(2, KT, P, 2, FJ, P).transpose(0, 4, 3, 2, 1, 5)
    small = np.concatenate([
        a(conv_w)[0].T.reshape(AB, P, CW).transpose(1, 0, 2).reshape(P, AB * CW),
        by_block(conv_b[0]), by_block(conv_ln_g[0]), by_block(conv_ln_b[0]),
        by_block(attn_norm[0]), by_block(attn_norm[1]), by_block(ffn_norm[0]), by_block(ffn_norm[1]),
        by_block(final_norm), by_block(lower_bounds[0]), by_block(lower_bounds[1]), by_block(c_norm_g[0])], axis=1)
    ins = {
        "x_t": x.T.reshape(KT, P, TOK).transpose(1, 0, 2).reshape(P, KT * TOK),
        "w_ab": tiles(w_in_ab[0]), "w_oab": tiles(w_out_ab[0]), "w_c": tiles(w_in_c[0]), "w_oc": tiles(w_out_c[0]),
        "w_fi": fi.reshape(4 * FJ, P, D), "w_fo": a(ffn_w_out).reshape(2 * FJ, P, D),
        "small": small, "rel": a(rel_bias)[0][:, ::-1],
        "k_cache": a(cache_a_k)[0].transpose(0, 2, 3, 1).reshape(NB, AB, P, CACHE).transpose(0, 2, 1, 3),
        "v_cache": a(cache_a_v)[0].reshape(NB, 4, P, AW).transpose(0, 2, 1, 3),
        "hist": a(state_conv)[0].transpose(2, 0, 1).reshape(AB, P, NB, HIST).transpose(1, 0, 2, 3),
        "state": a(state_hgrn)[0].transpose(1, 2, 0, 3),
    }
    outs = {
        "y": (P, KT * TOK), "k_new": (P, AB, CACHE + P), "v_new": (P, 5, AW), "conv_p": (P, AB, HIST),
        "conv_s": (P, AB, NB, HIST), "hg_p": (CH, P, P), "hg_s": (CH, P, NB, P),
    }
    nc = bacc.Bacc("TRN2", target_bir_lowering=False, num_devices=1)
    ins = {k: np.ascontiguousarray(v) for k, v in ins.items()}
    args = [nc.dram_tensor(k + "_in", v.shape, F32, kind="ExternalInput").ap() for k, v in ins.items()]
    args += [nc.dram_tensor(k + "_out", s, F32, kind="ExternalOutput").ap() for k, s in outs.items()]
    encoder(nc, *args)
    r = run_bass_kernel_spmd(nc, [{k + "_in": v for k, v in ins.items()}], core_ids=[0]).results[0]
    y, kn, vn, cp, cs, hp, hs = (r[k + "_out"] for k in outs)
    y = y.reshape(P, KT, TOK).transpose(2, 1, 0).reshape(TOK, D)
    kn = kn.transpose(2, 1, 0).reshape(CACHE + P, AH, AD)
    vn = vn.transpose(1, 0, 2).reshape(CACHE + P, AH, AD)
    return (y[:SEQ].reshape(1, SEQ, D), y[SEQ:].reshape(NB, NS, D),
            kn[:CACHE].reshape(1, 1, CACHE, AH, AD), vn[:CACHE].reshape(1, 1, CACHE, AH, AD),
            cp.transpose(2, 1, 0).reshape(1, 1, HIST, AW), hp.reshape(1, 1, CH, P, P),
            kn[CACHE:].reshape(1, NB, NS, AH, AD), vn[CACHE:].reshape(1, NB, NS, AH, AD),
            cs.transpose(2, 3, 1, 0).reshape(1, NB, HIST, AW),
            hs.transpose(2, 0, 1, 3).reshape(1, NB, CH, P, P))
```
